# Optimizing a Trainium2 kernel written in Bass

```python
import math
import jax, jax.numpy as jnp
from jax import lax
import numpy as np

D_MODEL = 1024
BATCH = 1
SEQ = 256
DEPTH = 1

GLA_HEADS = 4
GLA_DK = D_MODEL // 2
GLA_DV = D_MODEL
GLA_GATE_RANK = 16
GLA_TAU = 16.0
GLA_CHUNK = 64
DSA_HEADS = 8
DSA_HEAD_DIM = 128
DSA_LATENT = 256
IDX_HEADS = 8
IDX_DIM = 64
DSA_TOPK = 256
Q_BLOCK = 128
PEER_HEADS = 8
PEER_NKEYS = 128
PEER_NEXPERTS = PEER_NKEYS * PEER_NKEYS
PEER_DKEY = 256
PEER_TOPK = 16
PEER_TOKEN_BLOCK = 128
NORM_EPS = 1e-6

IN_SIZES = (GLA_DK, GLA_DK, GLA_DV, GLA_DV, GLA_GATE_RANK,
            DSA_HEADS * DSA_HEAD_DIM, DSA_LATENT, IDX_HEADS * IDX_DIM, IDX_DIM, IDX_HEADS,
            D_MODEL, D_MODEL)
IN_TOTAL = sum(IN_SIZES)


def _rmsnorm(x, g):
    x32 = x.astype(jnp.float32)
    y = x32 * lax.rsqrt(jnp.mean(x32 * x32, axis=-1, keepdims=True) + NORM_EPS)
    return (y * g.astype(jnp.float32)).astype(x.dtype)

def _alibi_slopes(n_heads):
    return jnp.exp2(-8.0 * jnp.arange(1, n_heads + 1, dtype=jnp.float32) / n_heads)

def _gla_chunked(q, k, v, log_alpha):
    B, H, S, dk = q.shape
    dv = v.shape[-1]
    C = GLA_CHUNK
    n = S // C
    q, k, v, la = [t.astype(jnp.float32).reshape(B, H, n, C, t.shape[-1]) for t in (q, k, v, log_alpha)]
    b = jnp.cumsum(la, axis=3)
    b_last = b[:, :, :, -1:, :]
    q_dec = q * jnp.exp(b)
    k_inv = k * jnp.exp(-b)
    k_end = k * jnp.exp(b_last - b)
    causal = jnp.tril(jnp.ones((C, C), dtype=bool))
    attn = jnp.where(causal, jnp.einsum('bhnid,bhnjd->bhnij', q_dec, k_inv), 0.0)
    o_intra = jnp.einsum('bhnij,bhnjv->bhniv', attn, v)

    def step(state, inp):
        q_c, k_c, v_c, decay_c = inp
        o_c = jnp.einsum('bhid,bhdv->bhiv', q_c, state)
        state = decay_c[..., None] * state + jnp.einsum('bhjd,bhjv->bhdv', k_c, v_c)
        return state, o_c

    xs = (jnp.moveaxis(q_dec, 2, 0), jnp.moveaxis(k_end, 2, 0), jnp.moveaxis(v, 2, 0),
          jnp.moveaxis(jnp.exp(b_last[:, :, :, 0, :]), 2, 0))
    state0 = jnp.zeros((B, H, dk, dv), jnp.float32)
    _, o_inter = lax.scan(step, state0, xs)
    o = o_intra + jnp.moveaxis(o_inter, 0, 2)
    return o.reshape(B, H, S, dv)

def _gla_branch(q, k, v, r, g_low, w_gate_up, b_gate, norm_g):
    B, S, _ = q.shape
    dkh = GLA_DK // GLA_HEADS
    dvh = GLA_DV // GLA_HEADS
    gate_logit = (g_low @ w_gate_up + b_gate).astype(jnp.float32)
    log_alpha = jax.nn.log_sigmoid(gate_logit) / GLA_TAU

    def heads(t, d):
        return t.reshape(B, S, GLA_HEADS, d).transpose(0, 2, 1, 3)

    o = _gla_chunked(heads(q, dkh) * (dkh ** -0.5), heads(k, dkh), heads(v, dvh), heads(log_alpha, dkh))
    o = o.transpose(0, 2, 1, 3)
    o = _rmsnorm(o, norm_g.reshape(GLA_HEADS, dvh)).reshape(B, S, GLA_DV)
    return o.astype(r.dtype) * jax.nn.silu(r)

def _dsa_branch(q, kv_raw, iq, ik, iw, kv_norm_g, w_uk, w_uv):
    B, S, _ = q.shape
    n_blocks = S // Q_BLOCK
    k_sel = min(DSA_TOPK, S // 4)
    c_kv = _rmsnorm(kv_raw, kv_norm_g)
    slopes = _alibi_slopes(DSA_HEADS)
    key_pos = jnp.arange(S, dtype=jnp.int32)

    def to_blocks(t):
        return t.reshape((B, n_blocks, Q_BLOCK) + t.shape[2:]).swapaxes(0, 1)

    q_b = to_blocks(q.reshape(B, S, DSA_HEADS, DSA_HEAD_DIM))
    iq_b = to_blocks(iq.reshape(B, S, IDX_HEADS, IDX_DIM))
    iw_b = to_blocks(iw)

    def block(inp):
        qb, iqb, iwb, blk = inp
        t = blk * Q_BLOCK + jnp.arange(Q_BLOCK, dtype=jnp.int32)
        rel = jax.nn.relu(jnp.einsum('bqhd,bsd->bqhs', iqb, ik).astype(jnp.float32) * (IDX_DIM ** -0.5))
        score = jnp.einsum('bqh,bqhs->bqs', iwb.astype(jnp.float32) * (IDX_HEADS ** -0.5), rel)
        score = jnp.where(key_pos[None, None, :] <= t[None, :, None], score, -jnp.inf)
        _, idx = lax.top_k(score, k_sel)
        kv_sel = jax.vmap(lambda cb, ib: cb[ib])(c_kv, idx)
        q_lat = jnp.einsum('bqhd,hdc->bqhc', qb, w_uk)
        logits = jnp.einsum('bqhc,bqkc->bqhk', q_lat, kv_sel).astype(jnp.float32) * (DSA_HEAD_DIM ** -0.5)
        dist = t[None, :, None] - idx
        logits = logits - slopes[None, None, :, None] * dist[:, :, None, :].astype(jnp.float32)
        logits = jnp.where((dist >= 0)[:, :, None, :], logits, -jnp.inf)
        p = jax.nn.softmax(logits, axis=-1).astype(kv_sel.dtype)
        o_lat = jnp.einsum('bqhk,bqkc->bqhc', p, kv_sel)
        o = jnp.einsum('bqhc,hcd->bqhd', o_lat, w_uv)
        return o.reshape(B, Q_BLOCK, DSA_HEADS * DSA_HEAD_DIM)

    out = lax.map(block, (q_b, iq_b, iw_b, jnp.arange(n_blocks, dtype=jnp.int32)))
    return out.swapaxes(0, 1).reshape(B, S, DSA_HEADS * DSA_HEAD_DIM)

def _peer(h, w_q, sub_keys_1, sub_keys_2, expert_u, expert_v):
    B, S, D = h.shape
    half = PEER_DKEY // 2
    q = (h @ w_q).reshape(B, S, PEER_HEADS, PEER_DKEY)
    s1 = jnp.einsum('bshd,nd->bshn', q[..., :half], sub_keys_1).astype(jnp.float32)
    s2 = jnp.einsum('bshd,nd->bshn', q[..., half:], sub_keys_2).astype(jnp.float32)
    v1, i1 = lax.top_k(s1, PEER_TOPK)
    v2, i2 = lax.top_k(s2, PEER_TOPK)
    cand = (v1[..., :, None] + v2[..., None, :]).reshape(B, S, PEER_HEADS, PEER_TOPK * PEER_TOPK)
    best, ci = lax.top_k(cand, PEER_TOPK)
    ia = jnp.take_along_axis(i1, ci // PEER_TOPK, axis=-1)
    ib = jnp.take_along_axis(i2, ci % PEER_TOPK, axis=-1)
    expert_idx = ia * PEER_NKEYS + ib
    gates = jax.nn.softmax(best, axis=-1)
    n_blocks = (B * S) // PEER_TOKEN_BLOCK
    h_b = h.reshape(n_blocks, PEER_TOKEN_BLOCK, D)
    i_b = expert_idx.reshape(n_blocks, PEER_TOKEN_BLOCK, PEER_HEADS, PEER_TOPK)
    g_b = gates.reshape(n_blocks, PEER_TOKEN_BLOCK, PEER_HEADS, PEER_TOPK)

    def block(inp):
        hx, ix, gx = inp
        u = expert_u[ix]
        v = expert_v[ix]
        a = jax.nn.gelu(jnp.einsum('td,thkd->thk', hx, u).astype(jnp.float32), approximate=False) * gx
        return jnp.einsum('thk,thkd->td', a.astype(hx.dtype), v)

    return lax.map(block, (h_b, i_b, g_b)).reshape(B, S, D)

def first_inputs(seed: int = 0) -> dict:
    key = jax.random.key(seed)
    ks = jax.random.split(key, 24)
    D = D_MODEL

    def nrm(k, shape, scale):
        return jax.random.normal(k, shape, jnp.float32) * scale

    def gain(k, shape):
        return 1.0 + 0.1 * jax.random.normal(k, shape, jnp.float32)

    return {
        "x": nrm(ks[0], (BATCH, SEQ, D), 1.0),
        "c": nrm(ks[1], (BATCH, D), 1.0),
        "w_ada": nrm(ks[2], (DEPTH, D, 6 * D), 0.5 * D ** -0.5),
        "b_ada": nrm(ks[3], (DEPTH, 6 * D), 0.02),
        "norm1_g": gain(ks[4], (DEPTH, D)),
        "w_in": nrm(ks[5], (DEPTH, D, IN_TOTAL), D ** -0.5),
        "gla_w_gate_up": nrm(ks[6], (DEPTH, GLA_GATE_RANK, GLA_DK), GLA_GATE_RANK ** -0.5),
        "gla_b_gate": nrm(ks[7], (DEPTH, GLA_DK), 0.1),
        "gla_norm_g": gain(ks[8], (DEPTH, GLA_DV)),
        "dsa_kv_norm_g": gain(ks[9], (DEPTH, DSA_LATENT)),
        "dsa_w_uk": nrm(ks[10], (DEPTH, DSA_HEADS, DSA_HEAD_DIM, DSA_LATENT), DSA_HEAD_DIM ** -0.5),
        "dsa_w_uv": nrm(ks[11], (DEPTH, DSA_HEADS, DSA_LATENT, DSA_HEAD_DIM), DSA_LATENT ** -0.5),
        "w_branch_a": nrm(ks[12], (DEPTH, GLA_DV, D), GLA_DV ** -0.5),
        "w_branch_b": nrm(ks[13], (DEPTH, DSA_HEADS * DSA_HEAD_DIM, D), (DSA_HEADS * DSA_HEAD_DIM) ** -0.5),
        "w_out": nrm(ks[14], (DEPTH, D, D), D ** -0.5),
        "norm2_g": gain(ks[15], (DEPTH, D)),
        "peer_w_q": nrm(ks[16], (DEPTH, D, PEER_HEADS * PEER_DKEY), D ** -0.5),
        "peer_sub_keys_1": nrm(ks[17], (DEPTH, PEER_NKEYS, PEER_DKEY // 2), (PEER_DKEY // 2) ** -0.5),
        "peer_sub_keys_2": nrm(ks[18], (DEPTH, PEER_NKEYS, PEER_DKEY // 2), (PEER_DKEY // 2) ** -0.5),
        "peer_u": nrm(ks[19], (DEPTH, PEER_NEXPERTS, D), D ** -0.5),
        "peer_v": nrm(ks[20], (DEPTH, PEER_NEXPERTS, D), PEER_HEADS ** -0.5),
        "final_norm_g": gain(ks[21], (D,)),
    }

def first_block(x, c, w_ada, b_ada, norm1_g, w_in, gla_w_gate_up, gla_b_gate, gla_norm_g,
              dsa_kv_norm_g, dsa_w_uk, dsa_w_uv, w_branch_a, w_branch_b, w_out, norm2_g,
              peer_w_q, peer_sub_keys_1, peer_sub_keys_2, peer_u, peer_v, final_norm_g):
    split_points = np.cumsum(IN_SIZES)[:-1].tolist()
    for l in range(DEPTH):
        ada = jax.nn.silu(c) @ w_ada[l] + b_ada[l]
        shift1, scale1, gate1, shift2, scale2, gate2 = jnp.split(ada[:, None, :], 6, axis=-1)

        h = _rmsnorm(x, norm1_g[l]) * (1.0 + scale1) + shift1
        proj = h @ w_in[l]
        (gq, gk, gv, gr, glow, dq, dkv, iq, ik, iw, za, zb) = jnp.split(proj, split_points, axis=-1)
        ya = _gla_branch(gq, gk, gv, gr, glow, gla_w_gate_up[l], gla_b_gate[l], gla_norm_g[l]) @ w_branch_a[l]
        yb = _dsa_branch(dq, dkv, iq, ik, iw, dsa_kv_norm_g[l], dsa_w_uk[l], dsa_w_uv[l]) @ w_branch_b[l]
        y = (jax.nn.sigmoid(za) * ya + jax.nn.sigmoid(zb) * yb) @ w_out[l]
        x = x + gate1 * y

        h2 = _rmsnorm(x, norm2_g[l]) * (1.0 + scale2) + shift2
        x = x + gate2 * _peer(h2, peer_w_q[l], peer_sub_keys_1[l], peer_sub_keys_2[l], peer_u[l], peer_v[l])
    return _rmsnorm(x, final_norm_g)


PLE_DIM = 256
D_CONF = D_MODEL // 2
D_SC = D_MODEL // 2
N_GROUPS_CONF = 8
N_GROUPS_SC = 8
CONF_KERNEL = 31
SC_KERNEL = 3
FFN_KERNEL = 3
D_FF = 2816
EPS = 1e-6

W_IN_COLS = 2 * D_CONF + 3 * D_SC + 2 * D_MODEL


def rmsnorm(x, g):
    xf = x.astype(jnp.float32)
    y = xf * lax.rsqrt(jnp.mean(xf * xf, axis=-1, keepdims=True) + EPS)
    return (y * g.astype(jnp.float32)).astype(x.dtype)

def layernorm(x, g, b):
    xf = x.astype(jnp.float32)
    mu = jnp.mean(xf, axis=-1, keepdims=True)
    var = jnp.mean(jnp.square(xf - mu), axis=-1, keepdims=True)
    y = (xf - mu) * lax.rsqrt(var + EPS)
    return (y * g.astype(jnp.float32) + b.astype(jnp.float32)).astype(x.dtype)

def causal_dwconv(u, w):
    k, c = w.shape
    return lax.conv_general_dilated(
        u, w[:, None, :].astype(u.dtype),
        window_strides=(1,), padding=[(k - 1, 0)],
        dimension_numbers=("NWC", "WIO", "NWC"),
        feature_group_count=c)

def second_inputs(seed: int = 0) -> dict:
    key = jax.random.key(seed)
    ks = jax.random.split(key, 24)
    f32 = jnp.float32

    def dense(k, shape, fan_in):
        return jax.random.normal(k, shape, f32) * (fan_in ** -0.5)

    def gain(k, shape):
        return 1.0 + 0.05 * jax.random.normal(k, shape, f32)

    def small(k, shape):
        return 0.02 * jax.random.normal(k, shape, f32)

    L = DEPTH
    return {
        "x": jax.random.normal(ks[0], (BATCH, SEQ, D_MODEL), f32),
        "p": jax.random.normal(ks[1], (DEPTH, BATCH, SEQ, PLE_DIM), f32),
        "g_mix": gain(ks[2], (L, D_MODEL)),
        "w_in": dense(ks[3], (L, D_MODEL, W_IN_COLS), D_MODEL),
        "b_gate": small(ks[4], (L, 2 * D_MODEL)),
        "conv_a_w": dense(ks[5], (L, CONF_KERNEL, D_CONF), CONF_KERNEL),
        "conv_a_b": small(ks[6], (L, D_CONF)),
        "ln_a_g": gain(ks[7], (L, D_CONF)),
        "ln_a_b": small(ks[8], (L, D_CONF)),
        "w_a_out": dense(ks[9], (L, D_CONF, D_MODEL), D_CONF),
        "conv_b_w": dense(ks[10], (L, SC_KERNEL, D_SC), SC_KERNEL),
        "w_b_out": dense(ks[11], (L, D_SC, D_MODEL), D_SC),
        "w_o": dense(ks[12], (L, D_MODEL, D_MODEL), D_MODEL),
        "g_ffn": gain(ks[13], (L, D_MODEL)),
        "w_up": dense(ks[14], (L, D_MODEL, 2 * D_FF), D_MODEL),
        "conv_f_w": dense(ks[15], (L, FFN_KERNEL, D_FF), FFN_KERNEL),
        "conv_f_b": small(ks[16], (L, D_FF)),
        "w_down": dense(ks[17], (L, D_FF, D_MODEL), D_FF),
        "g_ple": gain(ks[18], (L, D_MODEL)),
        "w_ple": dense(ks[19], (L, PLE_DIM, D_MODEL), PLE_DIM),
        "w_ple_gate": dense(ks[20], (L, D_MODEL, D_MODEL), D_MODEL),
        "g_final": gain(ks[21], (D_MODEL,)),
    }

def second_block(x, p, g_mix, w_in, b_gate, conv_a_w, conv_a_b, ln_a_g, ln_a_b, w_a_out,
              conv_b_w, w_b_out, w_o, g_ffn, w_up, conv_f_w, conv_f_b, w_down,
              g_ple, w_ple, w_ple_gate, g_final):
    o1 = D_CONF
    o2 = o1 + D_CONF
    o3 = o2 + D_SC
    o4 = o3 + D_SC
    o5 = o4 + D_SC
    o6 = o5 + D_MODEL
    for i in range(DEPTH):
        h = rmsnorm(x, g_mix[i])
        z = jnp.einsum("bsd,dn->bsn", h, w_in[i])
        a_val, a_gt = z[..., :o1], z[..., o1:o2]
        sc_b, sc_c, sc_v = z[..., o2:o3], z[..., o3:o4], z[..., o4:o5]
        gate_logits = z[..., o5:] + b_gate[i]
        g_a = jax.nn.sigmoid(gate_logits[..., :D_MODEL])
        g_b = jax.nn.sigmoid(gate_logits[..., D_MODEL:])

        a = a_val * jax.nn.sigmoid(a_gt)
        a = causal_dwconv(a, conv_a_w[i]) + conv_a_b[i]
        a = jax.nn.silu(layernorm(a, ln_a_g[i], ln_a_b[i]))
        y_a = jnp.einsum("bsc,cd->bsd", a, w_a_out[i])

        s = sc_b * causal_dwconv(sc_c * sc_v, conv_b_w[i])
        y_b = jnp.einsum("bsc,cd->bsd", s, w_b_out[i])

        x = x + jnp.einsum("bsd,de->bse", g_a * y_a + g_b * y_b, w_o[i])

        h = rmsnorm(x, g_ffn[i])
        u = jnp.einsum("bsd,df->bsf", h, w_up[i])
        f_gate = causal_dwconv(u[..., :D_FF], conv_f_w[i]) + conv_f_b[i]
        f = jax.nn.gelu(f_gate, approximate=True) * u[..., D_FF:]
        x = x + jnp.einsum("bsf,fd->bsd", f, w_down[i])

        pg = jax.nn.sigmoid(jnp.einsum("bsd,de->bse", rmsnorm(x, g_ple[i]), w_ple_gate[i]))
        x = x + pg * jnp.einsum("bsk,kd->bsd", p[i], w_ple[i])

    return rmsnorm(x, g_final)


def setup_inputs(seed=0):
    out = dict(first_inputs(seed))
    for name, value in second_inputs(seed + 1).items():
        if name != "x":
            out[name + "_2"] = value
    return out


def reference(
    x, c, w_ada, b_ada, norm1_g, w_in, gla_w_gate_up, gla_b_gate, gla_norm_g, dsa_kv_norm_g,
    dsa_w_uk, dsa_w_uv, w_branch_a, w_branch_b, w_out, norm2_g, peer_w_q, peer_sub_keys_1,
    peer_sub_keys_2, peer_u, peer_v, final_norm_g, p_2, g_mix_2, w_in_2, b_gate_2, conv_a_w_2,
    conv_a_b_2, ln_a_g_2, ln_a_b_2, w_a_out_2, conv_b_w_2, w_b_out_2, w_o_2, g_ffn_2, w_up_2,
    conv_f_w_2, conv_f_b_2, w_down_2, g_ple_2, w_ple_2, w_ple_gate_2, g_final_2,
):
    x = first_block(
        x, c, w_ada, b_ada, norm1_g, w_in, gla_w_gate_up, gla_b_gate, gla_norm_g, dsa_kv_norm_g,
        dsa_w_uk, dsa_w_uv, w_branch_a, w_branch_b, w_out, norm2_g, peer_w_q, peer_sub_keys_1,
        peer_sub_keys_2, peer_u, peer_v, final_norm_g,
    )
    return second_block(
        x, p_2, g_mix_2, w_in_2, b_gate_2, conv_a_w_2, conv_a_b_2, ln_a_g_2, ln_a_b_2,
        w_a_out_2, conv_b_w_2, w_b_out_2, w_o_2, g_ffn_2, w_up_2, conv_f_w_2, conv_f_b_2,
        w_down_2, g_ple_2, w_ple_2, w_ple_gate_2, g_final_2,
    )


_drawn_inputs = setup_inputs


def setup_inputs(seed=0):
    import zlib

    import numpy as np

    out = dict(_drawn_inputs(seed))
    spreads = {}
    factors = {'gla_b_gate': 7.207,
     'gla_norm_g': 3.852,
     'dsa_kv_norm_g': 3.141,
     'b_gate_2': 8.0,
     'conv_a_b_2': 4.56,
     'ln_a_g_2': 3.478,
     'ln_a_b_2': 8.0,
     'conv_f_b_2': 6.11,
     'g_ple_2': 24.142}
    for name, (base, spread) in spreads.items():
        noise = np.random.default_rng([zlib.crc32(name.encode()), seed]).standard_normal(out[name].shape)
        drawn = base * np.exp(spread * noise) if base else spread * noise
        out[name] = __import__('jax').numpy.asarray(drawn.astype(out[name].dtype))
    for name, factor in factors.items():
        out[name] = (out[name] * factor).astype(out[name].dtype)
    return out
```

```python
from contextlib import ExitStack

import concourse.bass as bass
from concourse import mybir

F32 = mybir.dt.float32
U32 = mybir.dt.uint32
ALU = mybir.AluOpType
ACT = mybir.ActivationFunctionType
X = mybir.AxisListType.X

P = 128
T = 256
NT = T // P
D = 1024
KD = D // P
EPS = 1e-6
SLOTS = 3
SLOT = 8 * 528
BANKS = 4

GH, DK, DV, CH = 4, 128, 256, 64
TAU = 16.0
AH, LAT, IH, TOPK = 8, 256, 8, 64
OUT_OF = -1e30
TAKEN = -3e38
EH, EK, NKEY = 8, 16, 128
QUARTERS = 4
PER_Q = EK // QUARTERS
CK, CC = 31, 4
FB = 22

O_GQ, O_GK, O_GV, O_GR, O_LOW, O_DQ, O_KV, O_IQ, O_IK, O_IW, O_ZA, O_ZB = (
    0, 512, 1024, 2048, 3072, 3088, 4112, 4368, 4880, 4944, 4952, 5976)

ROWS = [("b_ada", 0, 0, 48), ("norm1_g", 0, 48, 8), ("gla_b_gate", 0, 56, 4), ("gla_norm_g", 0, 60, 8),
        ("dsa_kv_norm_g", 0, 68, 2), ("norm2_g", 0, 70, 8), ("final_norm_g", 0, 78, 8), ("c", 0, 86, 8),
        ("g_mix_2", 1, 0, 8), ("b_gate_2", 1, 8, 16), ("conv_a_b_2", 1, 24, 4), ("ln_a_g_2", 1, 28, 4),
        ("ln_a_b_2", 1, 32, 4), ("g_ffn_2", 1, 36, 8), ("conv_f_b_2", 1, 44, 22), ("g_ple_2", 1, 66, 8),
        ("g_final_2", 1, 74, 8), ("conv_b_w_2", 1, 82, 12),
        ("conv_a_w_2", 2, 0, 124), ("conv_f_w_2", 3, 0, 66)]
ROW_TILES = [94, 94, 124, 66]


def work_table():
    chunks, blocks = [], []

    def chunk(key, name, kt, col, n, k0=0):
        chunks.append((key, name, kt, k0, col, n))

    def block(key, engine, back=0):
        blocks.append((key, engine, len(chunks) - 1 - back))

    def ada(j):
        chunk(("ada", j), "w_ada", KD, 512 * j, 512)
        block(("ada", j), "V")

    for j in range(4):
        ada(j)
    for key, col in (("gq", O_GQ), ("gk", O_GK)):
        chunk((key, 0), "w_in", KD, col, 512)
        for b in range(4):
            block((key, b), "A")
    for j in range(2):
        chunk(("gv", j), "w_in", KD, O_GV + 512 * j, 512)
        for t in range(NT):
            block(("gv", j, t), "A")
    chunk(("low", 0), "w_in", KD, O_LOW, 528)
    block(("low", 0), "A")
    for b in range(4):
        block(("dq", b), "A")
    chunk(("dq", 1), "w_in", KD, O_DQ + 512, 512)
    for b in range(4, 8):
        block(("dq", b), "A")
    chunk(("kv", 0), "w_in", KD, O_KV, 512)
    for b in range(2):
        block(("kv", b), "A")
    for b in range(2):
        block(("iq", b), "A")
    chunk(("iq", 1), "w_in", KD, O_IQ + 256, 328)
    for b in range(2, 4):
        block(("iq", b), "A")
    for b in range(2):
        block(("ik", b), "A")
    for t in range(NT):
        block(("iw", t), "A")
    for j in range(2):
        chunk(("gr", j), "w_in", KD, O_GR + 512 * j, 512)
        for b in range(4):
            block(("gr", 4 * j + b), "A")
    for h in range(AH):
        key, b = ("za", 2 * h) if h < 4 else ("zb", 2 * h - 8)
        if h % 2 == 0:
            chunk((key, b // 4), "w_in", KD, (O_ZA if h < 4 else O_ZB) + 128 * b, 512)
            for i in range(2):
                block((key, b + i), "A")
            ada(4 + h)
        else:
            ada(4 + h)
            for i in range(2):
                block((key, b + i), "A", back=2)
    for key, name in (("ba", "w_branch_a"), ("bb", "w_branch_b"), ("wo", "w_out")):
        for j in range(2):
            chunk((key, j), name, KD, 512 * j, 512)
            for b in range(4):
                block((key, 4 * j + b), "V")
    for j in range(4):
        chunk(("pq", j), "peer_w_q", KD, 512 * j, 512)
        for b in range(4):
            block(("pq", 4 * j + b), "A")
    for j in range(9):
        chunk(("z", j), "w_in_2", KD, 512 * j, 512)
        for b in range(4):
            block(("z", 4 * j + b), "A")
    for key, name in (("ya", "w_a_out_2"), ("yb", "w_b_out_2")):
        chunk((key, 0), name, CC, 0, D)
        for b in range(8):
            block((key, b), "V")
    for j in range(2):
        chunk(("o", j), "w_o_2", KD, 512 * j, 512)
        for b in range(4):
            block(("o", 4 * j + b), "V")
    for j in range(11):
        chunk(("up", j), "w_up_2", KD, 512 * j, 512)
        for b in range(4):
            block(("up", 4 * j + b), "A" if 4 * j + b < FB else "V")
    for j in range(4):
        for half in range(2):
            chunk(("down", j, half), "w_down_2", FB // 2, 256 * j, 256, half * FB // 2)
        for b in range(2):
            block(("down", 2 * j + b), "V")
    for j in range(2):
        chunk(("pg", j), "w_ple_gate_2", KD, 512 * j, 512)
        for b in range(4):
            block(("pg", 4 * j + b), "A")
    chunk(("pl", 0), "w_ple_2", 2, 0, D)
    for b in range(8):
        block(("pl", b), "V")
    return chunks, blocks


CHUNKS, BLOCKS = work_table()
CHUNK_AT = {c[0]: n for n, c in enumerate(CHUNKS)}
BLOCK_AT = {b[0]: n for n, b in enumerate(BLOCKS)}


def taken_by(engine, n):
    return sum(e == engine for _, e, _ in BLOCKS[:n + 1])


def last_product(c):
    key = CHUNKS[c][0]
    if key[0] == "down" and key[2] == 0:
        c += 1
    return max(n for n, (_, _, at) in enumerate(BLOCKS) if at == c)


def chunk_of(n):
    return BLOCKS[n][2]


INPUTS = ["x", "c", "w_ada", "b_ada", "norm1_g", "w_in", "gla_w_gate_up", "gla_b_gate", "gla_norm_g",
          "dsa_kv_norm_g", "dsa_w_uk", "dsa_w_uv", "w_branch_a", "w_branch_b", "w_out", "norm2_g",
          "peer_w_q", "peer_sub_keys_1", "peer_sub_keys_2", "peer_u", "peer_v", "final_norm_g", "p_2",
          "g_mix_2", "w_in_2", "b_gate_2", "conv_a_w_2", "conv_a_b_2", "ln_a_g_2", "ln_a_b_2",
          "w_a_out_2", "conv_b_w_2", "w_b_out_2", "w_o_2", "g_ffn_2", "w_up_2", "conv_f_w_2",
          "conv_f_b_2", "w_down_2", "g_ple_2", "w_ple_2", "w_ple_gate_2", "g_final_2"]


def rows_of(ap):
    n = len(ap.shape)
    if n == 1:
        return ap.rearrange("(r p) -> r p", p=P)
    if n == 2:
        return ap.rearrange("a (r p) -> (a r) p", p=P)
    return ap.rearrange("a b (r p) -> (a b r) p", p=P)


def two_blocks(nc, w, out):
    with ExitStack() as ctx:
        made = {}

        def S(name):
            if name not in made:
                made[name] = ctx.enter_context(nc.semaphore(name))
            return made[name]

        def sb(name, shape, dt=F32):
            return ctx.enter_context(nc.sbuf_tensor(name, shape, dt))

        ps = ctx.enter_context(nc.psum_tensor("ps", [P, 8, 512], F32))
        BK = [ps[:, b, :] for b in range(8)]

        ident, ones, epsc = sb("ident", [P, P]), sb("ones", [P, P]), sb("epsc", [P, 1])
        iota16 = sb("iota16", [P, EK])
        negdist = sb("negdist", [P, NT, T])
        vec = sb("vec", [P, 4, P])
        keyT = sb("keyT", [P, 2, P])
        csil = sb("csil", [P, KD])
        adaT = sb("adaT", [P, 48])
        mod = sb("mod", [P, KD])
        wring = sb("wring", [P, SLOTS, SLOT])
        xT, hT, sq = sb("xT", [P, KD, T]), sb("hT", [P, KD, T]), sb("sq", [P, KD, T])
        stat = sb("stat", [P, 2, T])
        SIZE = 32080
        arena = sb("arena", [P, SIZE])
        at = [0]

        def view(*dims):
            n = 1
            for d in dims:
                n *= d
            a = arena[:, at[0]:at[0] + n]
            at[0] += n
            assert at[0] <= SIZE, at[0]
            if len(dims) == 2:
                a = a.rearrange("p (a b) -> p a b", b=dims[1])
            if len(dims) == 3:
                a = a.rearrange("p (a b c) -> p a b c", b=dims[1], c=dims[2])
            if len(dims) == 4:
                a = a.rearrange("p (a b c d) -> p a b c d", b=dims[1], c=dims[2], d=dims[3])
            return a

        def again(start, *dims):
            at[0] = start
            return view(*dims)

        def col(name, i):
            t, r = next((t, r) for n, t, r, _ in ROWS if n == name)
            return vec[:, t, r + i:r + i + 1]

        def cols(name, n):
            t, r = next((t, r) for m, t, r, _ in ROWS if m == name)
            return vec[:, t, r:r + n]

        a_x = at[0]
        xtok = view(NT, D)
        a_qk = at[0]
        gq, gk = view(GH, T), view(GH, T)
        a_gv = at[0]
        gv = view(NT, D)
        low = view(T)
        dqT, kvT, iqT, ikT = view(AH, T), view(2, T), view(4, T), view(2, T)
        iw = view(NT, IH)
        gr, za, zb = view(KD, T), view(KD, T), view(KD, T)
        a_r1 = at[0]
        la, cum, ediff, ework = (view(GH * T) for _ in range(4))
        kendT = view(2 * GH, P)
        attn = view(2 * GH, P)
        gT = view(KD, T)
        wuv = view(AH, 2, P)
        scanmask = view(T)
        decay = view(GH * 4)
        ckv_tok = view(NT, LAT)
        madd = view(NT, T)
        a_score = at[0]
        score, work = view(T), view(T)
        m8 = view(8)
        rel, pr = view(2, T), view(2, T)
        pT = view(3, P)
        qlat, olat = view(2, T), view(2, T)
        sm = view(8)
        vrows = again(a_r1, 4, P)
        keyrows = view(2, P)
        wgate = again(a_score, 512)
        oT = again(a_x, KD, T)
        dsaT = again(a_qk, AH, T)
        comb = again(a_gv, KD, T)
        state = again(a_r1, 3, GH, DV)
        adarow = view(2, 512)
        ostd = again(a_score, GH * T)
        wuk = sq[:, :, :]

        at[0] = 0
        h2tok = view(NT, D)
        qs = view(4, T)
        s_all = view(NT * EH + 1, 2 * NKEY)
        pacc = view(NT, D)
        diag = view(EK, P)
        urows = view(EK, D)
        cur = view(2 * NKEY)
        cur2 = view(2 * NKEY)
        cand = view(EK, EK)
        cand2 = view(EK, EK)
        oneh = view(EK, EK)
        top = view(2, EK)
        topi = view(2, EK)
        best = view(EK)
        ci = view(2, EK)
        pick = view(2, EK)
        expb = view(EK)
        gst = view(4)
        dots = view(2, EK)
        gel = view(EK)
        amul = view(2, EK)
        topu = sb("topu", [P, 2, EK], U32)
        ciu = sb("ciu", [P, 3, EK], U32)
        rowid = sb("rowid", [P, 2, EK], U32)
        rows_in_ring = SLOTS * SLOT // D
        by_row = [a.rearrange("p a b -> p (a b)") for a in (wring[:, :, :], sq[:, :, :], hT[:, :, :])]
        vrows_e = [by_row[0][:, j * D:(j + 1) * D] for j in range(rows_in_ring)]
        vrows_e += [a[:, j * D:(j + 1) * D] for a in by_row[1:] for j in range(KD * T // D)]

        at[0] = 0
        ptok = view(NT, 256)
        pleT = view(2, T)
        apad = view(CC, CK - 1 + T)
        agate = view(CC, T)
        acc = view(CC, T)
        scb, scc = view(CC, T), view(CC, T)
        cpad = view(CC, 2 + T)
        sT = view(CC, T)
        zg = view(16, T)
        comb2 = view(KD, T)
        upad = view(FB, 2 + T)
        fT = view(FB, T)
        pgT = view(KD, T)
        otok = again(at[0] - KD * T - FB * T, NT, D)

        block = ctx.enter_context(nc.Block())

        def norm_names(tag):
            return tag + "_sq", tag + "_ss", tag + "_std", tag + "_h"

        @block.sync
        def _(sp):
            for name, t, r, k in ROWS[0:8]:
                sp.dma_start(vrows[r:r + k, t, :], rows_of(w[name])).then_inc(S("rows_in"), 16)

            def load(n):
                key, name, kt, k0, c0, nn = CHUNKS[n]
                if n >= SLOTS:
                    sp.wait_ge(S("product"), last_product(n - SLOTS) + 1)
                if key == ("z", 0):
                    sp.wait_ge(S("v_used"), NT * EH * EK)
                dst = wring[:, n % SLOTS, 0:kt * nn].rearrange("p (k n) -> p k n", n=nn)
                src = w[name][0].rearrange("(k p) n -> p k n", p=P)[:, k0:k0 + kt, c0:c0 + nn]
                sp.dma_start(dst, src).then_inc(S(f"chunk{n % SLOTS}"), 16)

            for n in range(len(CHUNKS)):
                load(n)
                if n == CHUNK_AT[("ada", 0)]:
                    sp.dma_start(xtok[:, :, :], w["x"][0].rearrange("(t p) d -> p t d", p=P)).then_inc(S("x_in"), 16)
                if n == CHUNK_AT[("gq", 0)]:
                    sp.wait_ge(S("n1_ss"), 1)
                    sp.dma_start(wuk.rearrange("p a b -> p (a b)").rearrange("p (h c) -> p h c", c=LAT),
                                 w["dsa_w_uk"][0].rearrange("h d c -> d h c")).then_inc(S("wuk_in"), 16)
                    sp.dma_start(wuv, w["dsa_w_uv"][0].rearrange("h (b c) d -> c h b d", c=P)).then_inc(S("wuv_in"), 16)
                if n == CHUNK_AT[("z", 2)]:
                    sp.dma_start(ptok[:, :, :], w["p_2"][0, 0].rearrange("(t p) d -> p t d", p=P)).then_inc(S("p_in"), 16)
            for t in range(NT):
                sp.wait_ge(S("out_cp"), 2 * (t + 1))
                sp.dma_start(out[0, t * P:(t + 1) * P, :], otok[:, t, :]).then_inc(S("stored"), 16)
            sp.wait_ge(S("stored"), 16 * NT)

        @block.gpsimd
        def _(pool):
            n_chain = [0]

            def link(ins, name=None):
                if name is None:
                    n_chain[0] += 1
                    ins.then_inc(S("pool_step"), 1)
                    pool.wait_ge(S("pool_step"), n_chain[0])
                else:
                    ins.then_inc(S(name), 1)

            link(pool.memset(ident[:, :], 0.0))
            link(pool.affine_select(out=ident[:, :], in_=ident[:, :], compare_op=ALU.not_equal, fill=1.0, base=0,
                                    pattern=[[-1, P]], channel_multiplier=1), "ident")
            pool.memset(ones[:, :], 1.0)
            link(pool.memset(epsc[:, :], EPS), "ones")
            link(pool.memset(scanmask, 1.0))
            link(pool.memset(scanmask.rearrange("p (n c) -> p n c", c=CH)[:, :, 0:1], 0.0))
            for t in range(NT):
                pool.iota(negdist[:, t, :], [[1, T]], base=-t * P, channel_multiplier=-1,
                          allow_small_or_imprecise_dtypes=True)
            link(pool.iota(iota16[:, :], [[1, EK]], base=0, channel_multiplier=0, allow_small_or_imprecise_dtypes=True))
            link(pool.memset(ikT[64:128, 0, :], 0.0))
            link(pool.memset(ikT[0:64, 1, :], 0.0))
            link(pool.memset(attn[:, :, :], 0.0), "pool_consts")

            for t in range(NT):
                nk = P * (t + 1)
                pool.wait_ge(S("index_sum"), IH * (t + 1))
                link(pool.affine_select(out=work[:, 0:nk], in_=score[:, 0:nk], compare_op=ALU.is_ge, fill=OUT_OF,
                                        base=t * P, pattern=[[-1, nk]], channel_multiplier=1), "causal")
                pool.wait_ge(S("picked"), t + 1)
                link(pool.affine_select(out=madd[:, t, 0:nk], in_=madd[:, t, 0:nk], compare_op=ALU.is_ge, fill=OUT_OF,
                                        base=t * P, pattern=[[-1, nk]], channel_multiplier=1), "madd_ready")
            pool.wait_ge(S("attn_cp"), 1)
            link(pool.affine_select(out=attn[:, :, :], in_=attn[:, :, :], compare_op=ALU.is_ge, fill=0.0, base=0,
                                    pattern=[[0, 2 * GH], [1, P]], channel_multiplier=-1), "attn_ready")

            U, Vx = w["peer_u"][0], w["peer_v"][0]

            def gather(g, j, even, table, dst, sem):
                pool.indirect_dma_start(out=dst, out_offset=None, in_=table,
                                        in_offset=bass.IndirectOffsetOnAxis(ap=rowid[:, even, j:j + 1], axis=0)
                                        ).then_inc(sem, 16)

            def head(g, even, first):
                pool.wait_ge(S("rows_ready"), g + 1)
                pool.sem_inc(S("pool_tick"), 1)
                for q in range(QUARTERS):
                    if not first:
                        pool.wait_ge(S("dot"), (g - 1) * EK + PER_Q * (q + 1))
                        pool.sem_inc(S("pool_tick"), 1)
                    for j in range(PER_Q * q, PER_Q * (q + 1)):
                        gather(g, j, even, U, urows[:, j, :], S(f"u_in{q}"))
                if first:
                    pool.wait_ge(S("product"), BLOCK_AT[("pq", 15)] + 1)
                for q in range(QUARTERS):
                    if not first:
                        pool.wait_ge(S("v_used"), (g - 1) * EK + PER_Q * (q + 1))
                        pool.sem_inc(S("pool_tick"), 1)
                    for j in range(PER_Q * q, PER_Q * (q + 1)):
                        gather(g, j, even, Vx, vrows_e[j], S(f"v_in{q}"))

            head(0, 0, True)
            with pool.Fori(1, EH - 1, 2) as g:
                head(g, 1, False)
                head(g + 1, 0, False)
            head(EH - 1, 1, False)
            head(EH, 0, False)
            with pool.Fori(EH + 1, 2 * EH - 1, 2) as g:
                head(g, 1, False)
                head(g + 1, 0, False)
            head(2 * EH - 1, 1, False)

        @block.tensor
        def _(pe):
            done = [0]

            def begin(key):
                n = BLOCK_AT[key]
                assert n == done[0], (key, n, done[0])
                done[0] += 1
                c = chunk_of(n)
                if n == 0 or chunk_of(n - 1) != c:
                    pe.wait_ge(S(f"chunk{c % SLOTS}"), 16 * (c // SLOTS + 1))
                if n >= BANKS:
                    e = BLOCKS[n - BANKS][1]
                    pe.wait_ge(S("taken_" + e), taken_by(e, n - BANKS))
                _, _, kt, _, _, nn = CHUNKS[c]
                return BK[n % BANKS], wring[:, c % SLOTS, 0:kt * nn].rearrange("p (k n) -> p k n", n=nn)

            def product(key, rhs, c0, m=P, kt=KD):
                bank, wt = begin(key)
                for k in range(kt):
                    mm = pe.matmul(bank[0:m, 0:T], wt[:, k, c0:c0 + m], rhs[:, k, :], start=k == 0, stop=k == kt - 1)
                mm.then_inc(S("product"), 1)

            def product_tok(key, t, c0, n):
                bank, wt = begin(key)
                for k in range(KD):
                    mm = pe.matmul(bank[:, 0:n], hT[:, k, t * P:(t + 1) * P], wt[:, k, c0:c0 + n],
                                   start=k == 0, stop=k == KD - 1)
                mm.then_inc(S("product"), 1)

            def ada(j):
                bank, wt = begin(("ada", j))
                for k in range(KD):
                    mm = pe.matmul(bank[0:1, :], csil[:, k:k + 1], wt[:, k, :], start=k == 0, stop=k == KD - 1)
                mm.then_inc(S("product"), 1)

            def ada_turned(j):
                pe.wait_ge(S("ada_row"), j + 1)
                for b in range(4):
                    mm = pe.matmul(BK[BLOCK_AT[("ada", j)] % BANKS][:, b:b + 1], adarow[0:1, j % 2, b * P:(b + 1) * P],
                                   ones[0:1, 0:1], start=True, stop=True)
                mm.then_inc(S("ada_mm"), 1)

            def sum_squares(tag, n=KD, src=sq, bank=4):
                pe.wait_ge(S(tag + "_sq"), 1)
                for k in range(n):
                    mm = pe.matmul(BK[bank][:, 0:T], ones[:, :], src[:, k, :], start=k == 0, stop=k == n - 1)
                mm.then_inc(S(tag + "_ss"), 1)

            pe.wait_ge(S("ident"), 1)
            pe.wait_ge(S("rows_in"), 16 * len(ROWS))
            for i, n in enumerate(ROW_TILES):
                mm = pe.transpose(BK[2][:, i * P:i * P + n], vrows[0:n, i, :], ident[0:n, 0:n])
            mm.then_inc(S("vec_mm"), 1)
            pe.wait_ge(S("keys_in"), 32)
            for i in range(2):
                mm = pe.transpose(BK[3][:, i * P:(i + 1) * P], keyrows[:, i, :], ident[:, :])
            mm.then_inc(S("key_mm"), 1)

            pe.wait_ge(S("ones"), 1)
            pe.wait_ge(S("csil"), 1)
            pe.wait_ge(S("vec"), 1)
            pe.wait_ge(S("keyT"), 1)
            ada(0)
            pe.wait_ge(S("x_in"), 16)
            for b in range(4):
                for k in (2 * b, 2 * b + 1):
                    for t in range(NT):
                        mm = pe.transpose(BK[4 + b][:, (k % 2) * T + t * P:(k % 2) * T + (t + 1) * P],
                                          xtok[:, t, k * P:(k + 1) * P], ident[:, :])
                mm.then_inc(S("x_mm"), 1)
            for j in range(1, 4):
                ada(j)
                ada_turned(j - 1)
                if j == 2:
                    pe.wait_ge(S("xT"), 4)
                    sum_squares("n1")
            ada_turned(3)

            pe.wait_ge(S("n1_h"), 1)
            for key in ("gq", "gk"):
                for b in range(4):
                    product((key, b), hT, b * P)
            for j in range(2):
                for t in range(NT):
                    product_tok(("gv", j, t), t, 0, 512)
            product(("low", 0), hT, 0, m=16)
            for b in range(8):
                product(("dq", b), hT, 16 + b * P if b < 4 else (b - 4) * P)
            for b in range(2):
                product(("kv", b), hT, b * P)
            for b in range(4):
                product(("iq", b), hT, 256 + b * P if b < 2 else (b - 2) * P)
            product(("ik", 0), hT, 256, m=64)
            product(("ik", 1), hT, 192)
            for t in range(NT):
                product_tok(("iw", t), t, 320, IH)

            pe.wait_ge(S("taken_A"), taken_by("A", BLOCK_AT[("low", 0)]))
            pe.wait_ge(S("wgate_in"), 16)
            for h in range(GH):
                mm = pe.matmul(BK[6 + h // 2][:, (h % 2) * T:(h % 2 + 1) * T], wgate[0:16, h * P:(h + 1) * P],
                               low[0:16, :], start=True, stop=True)
            mm.then_inc(S("gate_mm"), 1)
            sum_squares("kv", 2, rel)
            for b in range(2):
                product(("gr", b), hT, b * P)
            pe.wait_ge(S("kv_h"), 1)
            for t in range(NT):
                for b in range(2):
                    mm = pe.transpose(BK[5][:, t * LAT + b * P:t * LAT + (b + 1) * P], kvT[:, b, t * P:(t + 1) * P],
                                      ident[:, :])
            mm.then_inc(S("ckv_mm"), 1)

            pe.wait_ge(S("pool_consts"), 1)
            pe.wait_ge(S("taken_A"), taken_by("A", BLOCK_AT[("ik", 1)]))
            for t in range(NT):
                for h in range(IH):
                    i = t * IH + h
                    if i == 1:
                        pe.wait_ge(S("ckv_tok"), 1)
                    if i >= 2:
                        pe.wait_ge(S("rel"), i - 1)
                    pe.matmul(BK[4 + i % 2][:, 0:P * (t + 1)], iqT[:, h // 2, t * P:(t + 1) * P],
                              ikT[:, h % 2, 0:P * (t + 1)], start=True, stop=True).then_inc(S("index_mm"), 1)
            for b in range(2, 4):
                product(("gr", b), hT, b * P)

            pe.wait_ge(S("gla_in"), 1)
            for i in range(2):
                for j in range(4 * i, 4 * i + 4):
                    mm = pe.transpose(BK[6 + i][:, (j % 4) * P:(j % 4 + 1) * P], ediff[:, j * P:(j + 1) * P], ident[:, :])
                mm.then_inc(S("kend_mm"), 1)
            for b in range(4, 6):
                product(("gr", b), hT, (b - 4) * P)
            for i in range(2):
                pe.wait_ge(S("kendT"), i + 1)
                for j in range(4 * i, 4 * i + 4):
                    h, t = j // 2, j % 2
                    mm = pe.matmul(BK[6 + i][:, (j % 4) * P:(j % 4 + 1) * P], gk[:, h, t * P:(t + 1) * P],
                                   gq[:, h, t * P:(t + 1) * P], start=True, stop=True)
                mm.then_inc(S("attn_mm"), 1)
            for b in range(6, 8):
                product(("gr", b), hT, (b - 4) * P)
            pe.wait_ge(S("attn_cp"), 1)
            for n in range(3):
                t, half = n // 2, slice((n % 2) * CH, (n % 2 + 1) * CH)
                if n:
                    pe.wait_ge(S("state"), n)
                for h in range(GH):
                    mm = pe.matmul(BK[6 + h // 2][:, (h % 2) * DV:(h % 2 + 1) * DV], kendT[half, 2 * h + t, :],
                                   gv[half, t, h * DV:(h + 1) * DV], start=True, stop=True)
                mm.then_inc(S("update_mm"), 1)
            pe.wait_ge(S("state"), 3)
            pe.wait_ge(S("attn_ready"), 1)
            for h in range(GH):
                if h >= 2:
                    pe.wait_ge(S("o_cp"), h - 1)
                for b in range(2):
                    for t in range(NT):
                        o = BK[6 + h % 2][:, b * T + t * P:b * T + (t + 1) * P]
                        mm = pe.matmul(o, gv[:, t, h * DV + b * P:h * DV + (b + 1) * P], attn[:, 2 * h + t, :],
                                       start=True, stop=False, skip_group_check=True)
                        for n in (2 * t, 2 * t + 1):
                            if n:
                                c = (n % 2) * CH
                                mm = pe.matmul(o[:, c:c + CH], state[:, n - 1, h, b * P:(b + 1) * P],
                                               gq[:, h, t * P + c:t * P + c + CH], start=False, stop=n % 2 == 1,
                                               skip_group_check=True)
                mm.then_inc(S("o_mm"), 1)
            pe.wait_ge(S("o_sq"), GH)
            for h in range(GH):
                for b in range(2):
                    mm = pe.matmul(BK[6 + h // 2][:, (h % 2) * T:(h % 2 + 1) * T], ones[:, :], gT[:, 2 * h + b, :],
                                   start=b == 0, stop=b == 1)
            mm.then_inc(S("o_ss"), 1)

            pe.wait_ge(S("wuk_in"), 16)
            pe.wait_ge(S("wuv_in"), 16)
            pe.wait_ge(S("rel"), NT * IH)
            pe.wait_ge(S("o_std"), 1)
            wuk_h = wuk.rearrange("p a b -> p (a b)").rearrange("p (h c) -> p h c", c=LAT)
            for h in range(AH):
                if h:
                    pe.wait_ge(S("dsa_cp"), h)
                for b in range(2):
                    mm = pe.matmul(BK[4][:, b * T:(b + 1) * T], wuk_h[:, h, b * P:(b + 1) * P], dqT[:, h, :],
                                   start=True, stop=True)
                mm.then_inc(S("qlat_mm"), 1)
                if h % 2:
                    ada(4 + h)
                else:
                    product(("za" if h < 4 else "zb", 2 * h % 8), hT, 0)
                pe.wait_ge(S("qlat"), h + 1)
                for t in range(NT):
                    for b in range(2):
                        mm = pe.matmul(BK[5][:, t * P:t * P + P * (t + 1)], qlat[:, b, t * P:(t + 1) * P],
                                       kvT[:, b, 0:P * (t + 1)], start=b == 0, stop=b == 1)
                mm.then_inc(S("logit_mm"), 1)
                if h % 2:
                    product(("za" if h < 4 else "zb", 2 * h % 8), hT, 2 * P)
                    product(("za" if h < 4 else "zb", 2 * h % 8 + 1), hT, 3 * P)
                else:
                    product(("za" if h < 4 else "zb", 2 * h % 8 + 1), hT, P)
                    ada(4 + h)
                pe.wait_ge(S("p_ready"), h + 1)
                for i, (t, kt) in enumerate(((0, 0), (1, 0), (1, 1))):
                    mm = pe.transpose(BK[6][:, i * P:(i + 1) * P], pr[:, t, kt * P:(kt + 1) * P], ident[:, :])
                mm.then_inc(S("pT_mm"), 1)
                pe.wait_ge(S("pT"), h + 1)
                for b in range(2):
                    for t in range(NT):
                        for kt in range(t + 1):
                            mm = pe.matmul(BK[7][:, b * T + t * P:b * T + (t + 1) * P],
                                           ckv_tok[:, kt, b * P:(b + 1) * P], pT[:, t + kt, :],
                                           start=kt == 0, stop=kt == t)
                mm.then_inc(S("olat_mm"), 1)
                ada_turned(4 + h)
                pe.wait_ge(S("olat"), h + 1)
                for b in range(2):
                    mm = pe.matmul(BK[4][:, 0:T], wuv[:, h, b, :], olat[:, b, :], start=b == 0, stop=b == 1)
                mm.then_inc(S("dsa_mm"), 1)

            pe.wait_ge(S("gla_out"), 1)
            for b in range(8):
                product(("ba", b), gT, (b % 4) * P)
            pe.wait_ge(S("dsa_cp"), AH)
            for b in range(8):
                product(("bb", b), dsaT, (b % 4) * P)
            pe.wait_ge(S("comb"), 1)
            for b in range(8):
                product(("wo", b), comb, (b % 4) * P)
            sum_squares("n2")

            pe.wait_ge(S("n2_h"), 1)

            def head_scores(h):
                if h >= 4:
                    pe.wait_ge(S("scores"), h - 3)
                pe.wait_ge(S("taken_A"), taken_by("A", BLOCK_AT[("pq", 2 * h + 1)]))
                for half in range(2):
                    for t in range(NT):
                        mm = pe.matmul(BK[4 + h % 4][:, (2 * t + half) * P:(2 * t + half + 1) * P],
                                       qs[:, (2 * h + half) % 4, t * P:(t + 1) * P], keyT[:, half, :],
                                       start=True, stop=True)
                mm.then_inc(S("score_mm"), 1)

            for b in range(16):
                product(("pq", b), hT, (b % 4) * P)
                if b == 1:
                    for i in range(4):
                        for k in range(4 * (i % 2), 4 * (i % 2) + 4):
                            mm = pe.transpose(BK[4 + i][:, (k % 4) * P:(k % 4 + 1) * P],
                                              hT[:, k, (i // 2) * P:(i // 2 + 1) * P], ident[:, :])
                        mm.then_inc(S("h2_mm"), 1)
                    pe.wait_ge(S("h2tok"), 4)
                if b % 2 and b >= 3:
                    head_scores((b - 3) // 2)
            head_scores(7)

            def head(g, even, first):
                if not first:
                    pe.wait_ge(S("head_added"), g)
                for q in range(QUARTERS):
                    pe.wait_ge(S(f"v_in{q}"), 16 * PER_Q * (g + 1))
                    for j in range(PER_Q * q, PER_Q * (q + 1)):
                        if j % PER_Q == 0:
                            pe.wait_ge(S("diag"), g * EK + PER_Q * (q + 1))
                        for b in range(2):
                            mm = pe.matmul(BK[4 + 2 * even + b], diag[:, j, :], vrows_e[j][:, b * 512:(b + 1) * 512],
                                           start=j == 0, stop=j == EK - 1, skip_group_check=True)
                        mm.then_inc(S("v_used"), 1)

            pe.wait_ge(S("scores"), EH)
            head(0, 0, True)
            with pe.Fori(1, EH - 1, 2) as g:
                head(g, 1, False)
                head(g + 1, 0, False)
            head(EH - 1, 1, False)
            head(EH, 0, False)
            with pe.Fori(EH + 1, 2 * EH - 1, 2) as g:
                head(g, 1, False)
                head(g + 1, 0, False)
            head(2 * EH - 1, 1, False)
            pe.wait_ge(S("head_added"), NT * EH + 1)
            for b in range(4):
                for k in (2 * b, 2 * b + 1):
                    for t in range(NT):
                        mm = pe.transpose(BK[4 + b][:, (k % 2) * T + t * P:(k % 2) * T + (t + 1) * P],
                                          pacc[:, t, k * P:(k + 1) * P], ident[:, :])
                mm.then_inc(S("expert_mm"), 1)

            pe.wait_ge(S("expert_x"), 1)
            sum_squares("nf1")
            pe.wait_ge(S("nf1_h"), 1)
            sum_squares("nm")
            pe.wait_ge(S("nm_h"), 1)
            for b in range(36):
                product(("z", b), hT, (b % 4) * P)
                if b == 19:
                    pe.wait_ge(S("p_in"), 16)
                    for k in range(2):
                        for t in range(NT):
                            mm = pe.transpose(BK[7][:, k * T + t * P:k * T + (t + 1) * P],
                                              ptok[:, t, k * P:(k + 1) * P], ident[:, :])
                    mm.then_inc(S("ple_mm"), 1)

            pe.wait_ge(S("conv_a"), 1)
            for k in range(CC):
                mm = pe.matmul(BK[4][:, 0:T], ones[:, :], acc[:, k, :], start=k == 0, stop=k == CC - 1)
            mm.then_inc(S("ln_sum"), 1)
            pe.wait_ge(S("conv_b"), 1)
            sum_squares("ln", CC, sq, 5)
            pe.wait_ge(S("branch_a"), 1)
            for b in range(8):
                product(("ya", b), acc, b * P, kt=CC)
            for b in range(8):
                product(("yb", b), sT, b * P, kt=CC)
            pe.wait_ge(S("comb2"), 1)
            for b in range(8):
                product(("o", b), comb2, (b % 4) * P)
            sum_squares("nff")

            pe.wait_ge(S("nff_h"), 1)
            for b in range(2 * FB):
                product(("up", b), hT, (b % 4) * P)
            pe.wait_ge(S("ffn"), 1)
            for j in range(4):
                outs = []
                c = CHUNK_AT[("down", j, 0)]
                pe.wait_ge(S(f"chunk{c % SLOTS}"), 16 * (c // SLOTS + 1))
                for b in range(2):
                    bank, wt1 = begin(("down", 2 * j + b))
                    outs.append(bank)
                wt0 = wring[:, c % SLOTS, 0:FB // 2 * 256].rearrange("p (k n) -> p k n", n=256)
                for b in range(2):
                    for k in range(FB):
                        wt = wt0 if k < FB // 2 else wt1
                        mm = pe.matmul(outs[b][:, 0:T], wt[:, k % (FB // 2), b * P:(b + 1) * P], fT[:, k, :],
                                       start=k == 0, stop=k == FB - 1)
                    mm.then_inc(S("product"), 1)
            sum_squares("np")

            pe.wait_ge(S("np_h"), 1)
            for b in range(8):
                product(("pg", b), hT, (b % 4) * P)
            pe.wait_ge(S("pleT"), 1)
            for b in range(8):
                product(("pl", b), pleT, b * P, kt=2)
            sum_squares("nl")
            pe.wait_ge(S("nl_h"), 1)
            for t in range(NT):
                for i in range(2):
                    for k in range(4 * i, 4 * i + 4):
                        mm = pe.transpose(BK[4 + 2 * t + i][:, (k % 4) * P:(k % 4 + 1) * P],
                                          hT[:, k, t * P:(t + 1) * P], ident[:, :])
                    mm.then_inc(S("out_mm"), 1)

        @block.scalar
        def _(act):
            n_of = {}

            def link(ins, name="act_step"):
                n_of[name] = n_of.get(name, 0) + 1
                ins.then_inc(S(name), 1)
                act.wait_ge(S(name), n_of[name])

            taken = [0]

            def take(key, out, func=ACT.Copy, m=slice(0, P), n=T, **kw):
                b = BLOCK_AT[key]
                assert BLOCKS[b][1] == "A" and taken_by("A", b) == taken[0] + 1, key
                taken[0] += 1
                act.wait_ge(S("product"), b + 1)
                act.activation(out, BK[b % BANKS][m, 0:n], func, **kw).then_inc(S("taken_A"), 1)

            def square(tag, src, dst=sq, wait=None):
                if wait:
                    act.wait_ge(S(wait[0]), wait[1])
                act.activation(dst, src, ACT.Square).then_inc(S(tag + "_sq"), 1)

            def root(tag, n, bank=4):
                act.wait_ge(S(tag + "_ss"), 1)
                act.activation(stat[:, 0, :], BK[bank][:, 0:T], ACT.Sqrt, scale=1.0 / n,
                               bias=epsc[:, 0:1]).then_inc(S(tag + "_std"), 1)

            for name, t, r, k in ROWS[8:]:
                act.dma_start(vrows[r:r + k, t, :], rows_of(w[name])).then_inc(S("rows_in"), 16)
            act.dma_start(keyrows[:, 0, :], w["peer_sub_keys_1"][0]).then_inc(S("keys_in"), 16)
            act.dma_start(keyrows[:, 1, :], w["peer_sub_keys_2"][0]).then_inc(S("keys_in"), 16)
            act.dma_start(wgate[0:16, :], w["gla_w_gate_up"][0]).then_inc(S("wgate_in"), 16)

            act.wait_ge(S("vec"), 1)
            act.activation(csil[:, :], cols("c", KD), ACT.Silu).then_inc(S("csil"), 1)
            square("n1", xT[:, :, :], sq[:, :, :], ("xT", 4))
            act.wait_ge(S("ones"), 1)
            root("n1", D)

            for b in range(4):
                take(("gq", b), gq[:, b, :])
            for b in range(4):
                take(("gk", b), gk[:, b, :])
            for j in range(2):
                for t in range(NT):
                    take(("gv", j, t), gv[:, t, j * 512:(j + 1) * 512], n=512)
            take(("low", 0), low[0:16, :], m=slice(0, 16))
            for b in range(8):
                take(("dq", b), dqT[:, b, :])
            for b in range(2):
                take(("kv", b), kvT[:, b, :])
            for b in range(4):
                take(("iq", b), iqT[:, b, :])
                if b == 1:
                    act.wait_ge(S("taken_A"), taken[0])
                    square("kv", kvT[:, :, :], rel[:, :, :])
            take(("ik", 0), ikT[0:64, 0, :], m=slice(0, 64))
            take(("ik", 1), ikT[64:128, 1, :], m=slice(64, 128))
            for t in range(NT):
                take(("iw", t), iw[:, t, :], n=IH, scale=IH ** -0.5)

            act.wait_ge(S("gate_mm"), 1)
            for h in range(GH):
                ins = act.activation(la[:, h * T:(h + 1) * T], BK[6 + h // 2][:, (h % 2) * T:(h % 2 + 1) * T],
                                     ACT.Identity, bias=col("gla_b_gate", h))
            link(ins)
            link(act.activation(cum, la, ACT.Abs))
            link(act.activation(cum, cum, ACT.Exp, scale=-1.0))
            link(act.activation(cum, cum, ACT.Ln, bias=ones[:, 0:1]), "gate_ln")
            root("kv", LAT)
            for b in range(2):
                take(("gr", b), gr[:, b, :], ACT.Silu)
            act.wait_ge(S("gate_sum"), 1)
            act.activation(ework, cum, ACT.Exp, scale=1.0 / TAU)
            act.activation(la, cum, ACT.Exp, scale=-1.0 / TAU)
            act.activation(ediff, ediff, ACT.Exp, scale=1.0 / TAU).then_inc(S("gate_exp"), 1)

            for t in range(NT):
                for h in range(IH):
                    i = t * IH + h
                    act.wait_ge(S("index_mm"), i + 1)
                    if i >= 2:
                        act.wait_ge(S("index_sum"), i - 1)
                    act.activation(rel[:, i % 2, 0:P * (t + 1)], BK[4 + i % 2][:, 0:P * (t + 1)], ACT.Relu,
                                   scale=64 ** -0.5).then_inc(S("rel"), 1)
            for b in range(2, 4):
                take(("gr", b), gr[:, b, :], ACT.Silu)

            for i in range(2):
                act.wait_ge(S("kend_mm"), i + 1)
                act.activation(kendT[:, 4 * i:4 * i + 4, :].rearrange("p a b -> p (a b)"), BK[6 + i],
                               ACT.Copy).then_inc(S("kendT"), 1)
            for b in range(4, 6):
                take(("gr", b), gr[:, b, :], ACT.Silu)
            for i in range(2):
                act.wait_ge(S("attn_mm"), i + 1)
                if i == 0:
                    act.wait_ge(S("pool_consts"), 1)
                src = BK[6 + i].rearrange("p (a b) -> p a b", b=P)
                for c in range(2):
                    half = slice(c * CH, (c + 1) * CH)
                    ins = act.activation(attn[half, 4 * i:4 * i + 4, half], src[half, :, half], ACT.Copy)
            ins.then_inc(S("attn_cp"), 1)
            for b in range(6, 8):
                take(("gr", b), gr[:, b, :], ACT.Silu)
            for h in range(GH):
                act.wait_ge(S("o_mm"), h + 1)
                act.activation(oT[:, 2 * h:2 * h + 2, :].rearrange("p a b -> p (a b)"), BK[6 + h % 2],
                               ACT.Copy).then_inc(S("o_cp"), 1)
                act.wait_ge(S("o_cp"), h + 1)
                act.activation(gT[:, 2 * h:2 * h + 2, :], oT[:, 2 * h:2 * h + 2, :], ACT.Square).then_inc(S("o_sq"), 1)
            act.wait_ge(S("o_ss"), 1)
            for i in range(2):
                ins = act.activation(ostd[:, i * 512:(i + 1) * 512], BK[6 + i], ACT.Sqrt, scale=1.0 / DV,
                                     bias=epsc[:, 0:1])
            ins.then_inc(S("o_std"), 1)

            for h in range(AH):
                za_, b0 = (("za", za), ("zb", zb))[h // 4], 2 * h % 8
                act.wait_ge(S("qlat_mm"), h + 1)
                act.activation(qlat.rearrange("p a b -> p (a b)"), BK[4], ACT.Copy).then_inc(S("qlat"), 1)
                if h % 2 == 0:
                    take((za_[0], b0), za_[1][:, b0, :])
                act.wait_ge(S("logits"), h + 1)
                for t in range(NT):
                    ins = act.activation(pr[:, t, 0:P * (t + 1)], pr[:, t, 0:P * (t + 1)], ACT.Exp,
                                         bias=sm[:, 2 + t:3 + t], accum_out=sm[:, 4 + t:5 + t])
                ins.then_inc(S("p_exp"), 1)
                if h % 2:
                    take((za_[0], b0), za_[1][:, b0, :])
                take((za_[0], b0 + 1), za_[1][:, b0 + 1, :])
                act.wait_ge(S("pT_mm"), h + 1)
                act.activation(pT.rearrange("p a b -> p (a b)"), BK[6][:, 0:3 * P], ACT.Copy).then_inc(S("pT"), 1)
                act.wait_ge(S("olat_mm"), h + 1)
                act.activation(olat.rearrange("p a b -> p (a b)"), BK[7], ACT.Copy).then_inc(S("olat"), 1)
            act.wait_ge(S("taken_A"), taken[0])
            act.activation(za[:, :, :], za[:, :, :], ACT.Sigmoid)
            act.activation(zb[:, :, :], zb[:, :, :], ACT.Sigmoid).then_inc(S("gates"), 1)

            def soften(g):
                act.wait_ge(S("best"), g + 1)
                act.sem_inc(S("act_tick"), 1)
                act.activation(expb, best, ACT.Exp, bias=gst[:, 0:1], accum_out=gst[:, 1:2]).then_inc(S("best_exp"), 1)

            square("n2", xT[:, :, :], sq[:, :, :], ("x1", 1))
            root("n2", D)
            for b in range(16):
                if b == 2:
                    for i in range(4):
                        act.wait_ge(S("h2_mm"), i + 1)
                        act.activation(h2tok[:, i // 2, (i % 2) * 512:(i % 2 + 1) * 512], BK[4 + i],
                                       ACT.Copy).then_inc(S("h2tok"), 1)
                if b == 12:
                    soften(0)
                if b >= 4:
                    act.wait_ge(S("score_mm"), b // 2 - 1)
                take(("pq", b), qs[:, b % 4, :])

            def head(g, even, first, last=False):
                act.wait_ge(S("dot"), EK * (g + 1))
                act.sem_inc(S("act_tick"), 1)
                act.activation(gel, dots[:, even, :], ACT.Gelu).then_inc(S("gelu"), 1)
                act.wait_ge(S("weight"), g + 1)
                act.sem_inc(S("act_tick"), 1)
                for j in range(EK):
                    if not first and j % PER_Q == 0:
                        act.wait_ge(S("v_used"), (g - 1) * EK + j + PER_Q)
                        act.sem_inc(S("act_tick"), 1)
                    act.activation(diag[:, j, :], ident[:, :], ACT.Copy,
                                   scale=amul[:, even, j:j + 1]).then_inc(S("diag"), 1)
                if not last:
                    soften(g + 1)

            head(0, 0, True)
            with act.Fori(1, EH - 1, 2) as g:
                head(g, 1, False)
                head(g + 1, 0, False)
            head(EH - 1, 1, False)
            head(EH, 0, False)
            with act.Fori(EH + 1, 2 * EH - 1, 2) as g:
                head(g, 1, False)
                head(g + 1, 0, False)
            head(2 * EH - 1, 1, False, last=True)

            square("nf1", xT[:, :, :], sq[:, :, :], ("expert_x", 1))
            root("nf1", D)
            square("nm", xT[:, :, :], sq[:, :, :], ("nf1_h", 1))
            root("nm", D)

            act.wait_ge(S("pads"), 1)
            for b in range(4):
                take(("z", b), apad[:, b, CK - 1:])
            for b in range(4):
                take(("z", 4 + b), agate[:, b, :], ACT.Sigmoid)
            for b in range(4):
                take(("z", 8 + b), scb[:, b, :])
            for b in range(4):
                take(("z", 12 + b), scc[:, b, :])
            for b in range(4):
                take(("z", 16 + b), cpad[:, b, 2:])
            for b in range(16):
                take(("z", 20 + b), zg[:, b, :], ACT.Sigmoid, bias=col("b_gate_2", b))
                if b == 0:
                    act.wait_ge(S("ple_mm"), 1)
                    act.activation(pleT.rearrange("p a b -> p (a b)"), BK[7], ACT.Copy).then_inc(S("pleT"), 1)

            square("ln", acc[:, :, :], sq[:, 0:CC, :], ("ln_mean", 1))
            act.wait_ge(S("ln_ss"), 1)
            act.activation(stat[:, 0, :], BK[5][:, 0:T], ACT.Sqrt, scale=1.0 / 512,
                           bias=epsc[:, 0:1]).then_inc(S("ln_std"), 1)
            act.wait_ge(S("ln_norm"), 1)
            for b in range(CC):
                ins = act.activation(acc[:, b, :], acc[:, b, :], ACT.Silu, bias=col("ln_a_b_2", b))
            ins.then_inc(S("branch_a"), 1)

            square("nff", xT[:, :, :], sq[:, :, :], ("x3", 1))
            root("nff", D)
            def ffn_gelu(b):
                act.wait_ge(S("conv_f"), b + 1)
                act.activation(fT[:, b, :], fT[:, b, :], ACT.Gelu_apprx_tanh,
                               bias=col("conv_f_b_2", b)).then_inc(S("ffn_gelu"), 1)

            for b in range(FB):
                take(("up", b), upad[:, b, 2:])
                if b >= 2:
                    ffn_gelu(b - 2)
            ffn_gelu(FB - 2)
            ffn_gelu(FB - 1)

            square("np", xT[:, :, :], sq[:, :, :], ("x4", 1))
            root("np", D)
            for b in range(8):
                take(("pg", b), pgT[:, b, :], ACT.Sigmoid)
            square("nl", xT[:, :, :], sq[:, :, :], ("x5", 1))
            root("nl", D)
            for i in range(4):
                act.wait_ge(S("out_mm"), i + 1)
                act.activation(otok[:, i // 2, (i % 2) * 512:(i % 2 + 1) * 512], BK[4 + i],
                               ACT.Copy).then_inc(S("out_cp"), 1)

        @block.vector
        def _(v):
            n_of = {}

            def link(ins, name="vec_step"):
                n_of[name] = n_of.get(name, 0) + 1
                ins.then_inc(S(name), 1)
                v.wait_ge(S(name), n_of[name])

            def stt(out, in0, scalar, in1, op0=ALU.mult, op1=ALU.mult):
                return v.scalar_tensor_tensor(out=out, in0=in0, scalar=scalar, in1=in1, op0=op0, op1=op1)

            taken = [0]

            def arrived(key):
                b = BLOCK_AT[key]
                assert BLOCKS[b][1] == "V" and taken_by("V", b) == taken[0] + 1, key
                taken[0] += 1
                v.wait_ge(S("product"), b + 1)
                return BK[b % BANKS]

            def ada(j):
                v.wait_ge(S("product"), BLOCK_AT[("ada", j)] + 1)
                link(v.tensor_copy(adarow[0:1, j % 2, :], BK[BLOCK_AT[("ada", j)] % BANKS][0:1, :]), "ada_row")

            def ada_turned(j):
                bank = arrived(("ada", j))
                v.wait_ge(S("ada_mm"), j + 1)
                link(v.tensor_tensor(adaT[:, 4 * j:4 * j + 4], bank[:, 0:4], cols("b_ada", 48)[:, 4 * j:4 * j + 4],
                                     ALU.add), "taken_V")

            def normed(tag, out, gain, n=KD, shift=None, src=xT):
                v.wait_ge(S(tag + "_std"), 1)
                link(v.reciprocal(stat[:, 1, :], stat[:, 0, :]))
                for k in range(n):
                    ins = stt(out[:, k, :], src[:, k, :], gain(k), stat[:, 1, :])
                if shift:
                    link(ins)
                    for k in range(n):
                        ins = v.tensor_scalar(out[:, k, :], out[:, k, :], shift(k), None, ALU.add)
                link(ins, tag + "_h")

            v.wait_ge(S("vec_mm"), 1)
            for i, n in enumerate(ROW_TILES):
                ins = v.tensor_copy(vec[:, i, 0:n], BK[2][:, i * P:i * P + n])
            link(ins, "vec")
            v.wait_ge(S("key_mm"), 1)
            link(v.tensor_copy(keyT[:, :, :],
                               BK[3][:, 0:2 * P].rearrange("p (a b) -> p a b", b=P)), "keyT")
            ada(0)
            for b in range(4):
                v.wait_ge(S("x_mm"), b + 1)
                link(v.tensor_copy(xT[:, 2 * b:2 * b + 2, :], BK[4 + b].rearrange("p (a b) -> p a b", b=T)), "xT")
            for j in range(1, 4):
                ada(j)
                ada_turned(j - 1)
            ada_turned(3)
            link(stt(mod[:, :], adaT[:, 8:16], 1.0, cols("norm1_g", KD), ALU.add, ALU.mult))
            normed("n1", hT, lambda k: mod[:, k:k + 1], shift=lambda k: adaT[:, k:k + 1])

            v.wait_ge(S("gate_ln"), 1)
            v.wait_ge(S("pool_consts"), 1)
            link(v.tensor_scalar(la, la, 0.0, None, ALU.min))
            link(v.tensor_tensor(la, la, cum, ALU.subtract))
            for h in range(GH):
                ins = v.tensor_tensor_scan(cum[:, h * T:(h + 1) * T], scanmask, la[:, h * T:(h + 1) * T], 0.0,
                                           ALU.mult, ALU.add)
            link(ins)
            by_chunk = [a.rearrange("p (n c) -> p n c", c=CH) for a in (cum, ediff, ework)]
            link(v.tensor_tensor(by_chunk[1], by_chunk[0][:, :, CH - 1:CH].broadcast_to([P, 4 * GH, CH]), by_chunk[0],
                                 ALU.subtract), "gate_sum")
            normed("kv", kvT, lambda k: col("dsa_kv_norm_g", k), n=2, src=kvT)
            v.wait_ge(S("gate_exp"), 1)
            v.wait_ge(S("taken_A"), taken_by("A", BLOCK_AT[("gk", 3)]))
            flat = lambda a: a.rearrange("p a b -> p (a b)")
            v.tensor_copy(decay.rearrange("p (n c) -> p n c", c=1), by_chunk[2][:, :, CH - 1:CH])
            stt(flat(gq), flat(gq), DK ** -0.5, ework)
            v.tensor_tensor(ediff, flat(gk), ediff, ALU.mult)
            link(v.tensor_tensor(flat(gk), flat(gk), la, ALU.mult), "gla_in")
            v.wait_ge(S("ckv_mm"), 1)
            link(v.tensor_copy(ckv_tok[:, :, :], BK[5].rearrange("p (a b) -> p a b", b=LAT)), "ckv_tok")

            v.wait_ge(S("taken_A"), taken_by("A", BLOCK_AT[("iw", NT - 1)]))
            v.wait_ge(S("gate_mm"), 1)
            for t in range(NT):
                nk = P * (t + 1)
                if t:
                    v.wait_ge(S("causal"), t)
                for h in range(IH):
                    i = t * IH + h
                    v.wait_ge(S("rel"), i + 1)
                    if h == 0:
                        ins = v.tensor_scalar(score[:, 0:nk], rel[:, i % 2, 0:nk], iw[:, t, h:h + 1], None, ALU.mult)
                    else:
                        ins = stt(score[:, 0:nk], rel[:, i % 2, 0:nk], iw[:, t, h:h + 1], score[:, 0:nk],
                                  ALU.mult, ALU.add)
                    link(ins, "index_sum")
                v.wait_ge(S("causal"), t + 1)
                for r in range(TOPK // 8):
                    link(v.max(m8, work[:, 0:nk]))
                    link(v.match_replace(work[:, 0:nk], m8, work[:, 0:nk], TAKEN))
                link(v.tensor_scalar(madd[:, t, 0:nk], work[:, 0:nk], 0.5 * TAKEN, OUT_OF, ALU.is_ge, ALU.mult), "picked")

            for n in range(3):
                v.wait_ge(S("update_mm"), n + 1)
                for h in range(GH):
                    u = BK[6 + h // 2][:, (h % 2) * DV:(h % 2 + 1) * DV]
                    if n == 0:
                        ins = v.tensor_copy(state[:, 0, h, :], u)
                    else:
                        ins = stt(state[:, n, h, :], state[:, n - 1, h, :], decay[:, 4 * h + n:4 * h + n + 1], u,
                                  ALU.mult, ALU.add)
                link(ins, "state")
            v.wait_ge(S("o_std"), 1)
            link(v.reciprocal(ostd, ostd))
            v.wait_ge(S("taken_A"), taken_by("A", BLOCK_AT[("gr", 7)]))
            for b in range(8):
                ins = stt(oT[:, b, :], oT[:, b, :], col("gla_norm_g", b), ostd[:, (b // 2) * T:(b // 2 + 1) * T])
            link(ins)
            link(v.tensor_tensor(flat(gT), flat(oT), flat(gr), ALU.mult), "gla_out")

            v.wait_ge(S("madd_ready"), NT)
            for h in range(AH):
                for t in range(NT):
                    nk = P * (t + 1)
                    ins = stt(rel[:, t, 0:nk], negdist[:, t, 0:nk], 2.0 ** -(h + 1), madd[:, t, 0:nk], ALU.mult, ALU.add)
                link(ins)
                v.wait_ge(S("logit_mm"), h + 1)
                for t in range(NT):
                    nk = P * (t + 1)
                    ins = stt(pr[:, t, 0:nk], BK[5][:, t * P:t * P + nk], P ** -0.5, rel[:, t, 0:nk], ALU.mult, ALU.add)
                link(ins)
                for t in range(NT):
                    ins = v.tensor_reduce(sm[:, t:t + 1], pr[:, t, 0:P * (t + 1)], X, ALU.max)
                link(ins)
                link(v.tensor_scalar(sm[:, 2:4], sm[:, 0:2], -1.0, None, ALU.mult), "logits")
                v.wait_ge(S("p_exp"), h + 1)
                link(v.reciprocal(sm[:, 6:8], sm[:, 4:6]))
                for t in range(NT):
                    nk = P * (t + 1)
                    ins = v.tensor_scalar(pr[:, t, 0:nk], pr[:, t, 0:nk], sm[:, 6 + t:7 + t], None, ALU.mult)
                link(ins, "p_ready")
                ada(4 + h)
                ada_turned(4 + h)
                v.wait_ge(S("dsa_mm"), h + 1)
                link(v.tensor_copy(dsaT[:, h, :], BK[4][:, 0:T]), "dsa_cp")

            v.wait_ge(S("gates"), 1)
            for b in range(8):
                link(v.tensor_tensor(comb[:, b, :], arrived(("ba", b))[:, 0:T], za[:, b, :], ALU.mult), "taken_V")
            for b in range(8):
                link(v.tensor_tensor(zb[:, b, :], arrived(("bb", b))[:, 0:T], zb[:, b, :], ALU.mult), "taken_V")
            link(v.tensor_tensor(flat(comb), flat(comb), flat(zb), ALU.add), "comb")
            for b in range(8):
                link(stt(xT[:, b, :], arrived(("wo", b))[:, 0:T], adaT[:, 16 + b:17 + b], xT[:, b, :], ALU.mult, ALU.add),
                     "taken_V")
            v.sem_inc(S("x1"), 1)
            link(stt(mod[:, :], adaT[:, 32:40], 1.0, cols("norm2_g", KD), ALU.add, ALU.mult))
            normed("n2", hT, lambda k: mod[:, k:k + 1], shift=lambda k: adaT[:, 24 + k:25 + k])

            def by(body):
                n = [0]

                def step(ins):
                    n[0] += 1
                    ins.then_inc(S("head_step"), 1)
                    v.wait_ge(S("head_step"), n[0])

                body(step)
                v.sem_inc(S("head_step"), -n[0])

            def route(g, even):
                def body(step):
                    step(v.tensor_copy(cur, s_all[:, bass.ds(g, 1), :].rearrange("p a b -> p (a b)")
                                       if not isinstance(g, int) else s_all[:, g, :]))
                    for i in range(2):
                        half, half2 = cur[:, i * NKEY:(i + 1) * NKEY], cur2[:, i * NKEY:(i + 1) * NKEY]
                        step(v.max(top[:, i, 0:8], half))
                        v.max_index(topu[:, i, 0:8], top[:, i, 0:8], half)
                        step(v.match_replace(half2, top[:, i, 0:8], half, TAKEN))
                        step(v.max(top[:, i, 8:16], half2))
                        step(v.max_index(topu[:, i, 8:16], top[:, i, 8:16], half2))
                    v.tensor_copy(topi[:, :, :], topu[:, :, :])
                    step(v.tensor_tensor(cand, top[:, 0, :].rearrange("p (a b) -> p a b", b=1).broadcast_to([P, EK, EK]),
                                         top[:, 1, :].rearrange("p (b a) -> p b a", b=1).broadcast_to([P, EK, EK]),
                                         ALU.add))
                    cf, cf2 = cand.rearrange("p a b -> p (a b)"), cand2.rearrange("p a b -> p (a b)")
                    step(v.max(best[:, 0:8], cf))
                    v.max_index(ciu[:, 0, 0:8], best[:, 0:8], cf)
                    step(v.match_replace(cf2, best[:, 0:8], cf, TAKEN))
                    step(v.max(best[:, 8:16], cf2))
                    step(v.max_index(ciu[:, 0, 8:16], best[:, 8:16], cf2))
                    v.tensor_scalar(gst[:, 0:1], best[:, 0:1], -1.0, None, ALU.mult).then_inc(S("best"), 1)
                    v.tensor_scalar(ciu[:, 1, :], ciu[:, 0, :], 4, None, ALU.logical_shift_right)
                    step(v.tensor_scalar(ciu[:, 2, :], ciu[:, 0, :], EK - 1, None, ALU.bitwise_and))
                    step(v.tensor_copy(ci[:, :, :], ciu[:, 1:3, :]))
                    for i in range(2):
                        step(v.tensor_tensor(oneh, iota16[:, :].rearrange("p (b a) -> p b a", b=1).broadcast_to([P, EK, EK]),
                                             ci[:, i, :].rearrange("p (a b) -> p a b", b=1).broadcast_to([P, EK, EK]),
                                             ALU.is_equal))
                        step(v.tensor_tensor(oneh, oneh,
                                             topi[:, i, :].rearrange("p (b a) -> p b a", b=1).broadcast_to([P, EK, EK]),
                                             ALU.mult))
                        step(v.tensor_reduce(pick[:, i, :], oneh, X, ALU.add))
                    step(stt(pick[:, 0, :], pick[:, 0, :], float(NKEY), pick[:, 1, :], ALU.mult, ALU.add))
                    v.tensor_copy(rowid[:, even, :], pick[:, 0, :]).then_inc(S("rows_ready"), 1)
                by(body)

            def dot(g, even, t, q):
                v.wait_ge(S(f"u_in{q}"), 16 * PER_Q * (g + 1))
                v.sem_inc(S("vec_tick"), 1)
                for j in range(PER_Q * q, PER_Q * (q + 1)):
                    v.tensor_tensor_reduce(out=urows[:, j, :], in0=urows[:, j, :], in1=h2tok[:, t, :], scale=1.0,
                                           scalar=0.0, op0=ALU.mult, op1=ALU.add,
                                           accum_out=dots[:, even, j:j + 1]).then_inc(S("dot"), 1)

            def weigh(g, even):
                v.wait_ge(S("best_exp"), g + 1)
                v.sem_inc(S("vec_tick"), 1)
                by(lambda step: step(v.reciprocal(gst[:, 2:3], gst[:, 1:2])))
                v.wait_ge(S("gelu"), g + 1)
                v.sem_inc(S("vec_tick"), 1)
                stt(amul[:, even, :], gel, gst[:, 2:3], expb).then_inc(S("weight"), 1)

            def add(g, even, t):
                v.wait_ge(S("v_used"), EK * (g + 1))
                v.sem_inc(S("vec_tick"), 1)
                v.wait_ge(S("head_added"), g + 1)
                acc_t = pacc[:, t, :].rearrange("p (a b) -> p a b", b=512)
                v.tensor_tensor(acc_t, ps[:, 4 + 2 * even:6 + 2 * even, :], acc_t, ALU.add).then_inc(S("head_added"), 1)

            def head(g, even, t, last=False, add_to=None):
                for q in range(QUARTERS):
                    dot(g, even, t, q)
                add(g - 1, 1 - even, t if add_to is None else add_to)
                weigh(g, even)
                if not last:
                    route(g + 1, 1 - even)

            v.memset(s_all[:, NT * EH, :], 0.0)
            link(v.memset(pacc[:, :, :], 0.0), "head_added")

            def scores(h):
                v.wait_ge(S("score_mm"), h + 1)
                link(v.tensor_copy(s_all[:, h:h + EH + 1:EH, :], BK[4 + h % 4].rearrange("p (t n) -> p t n", n=2 * NKEY)),
                     "scores")

            scores(0)
            route(0, 0)
            for h in range(1, 4):
                scores(h)
            v.wait_ge(S("h2tok"), 4)
            for q in range(QUARTERS):
                scores(4 + q)
                dot(0, 0, 0, q)
            weigh(0, 0)
            route(1, 1)
            with v.Fori(1, EH - 1, 2) as g:
                head(g, 1, 0)
                head(g + 1, 0, 0)
            head(EH - 1, 1, 0)
            head(EH, 0, 1, add_to=0)
            with v.Fori(EH + 1, 2 * EH - 1, 2) as g:
                head(g, 1, 1)
                head(g + 1, 0, 1)
            head(2 * EH - 1, 1, 1, last=True)
            add(2 * EH - 1, 1, 1)
            for b in range(4):
                v.wait_ge(S("expert_mm"), b + 1)
                for k in (2 * b, 2 * b + 1):
                    ins = stt(xT[:, k, :], BK[4 + b][:, (k % 2) * T:(k % 2 + 1) * T], adaT[:, 40 + k:41 + k],
                              xT[:, k, :], ALU.mult, ALU.add)
            link(ins, "expert_x")
            normed("nf1", xT, lambda k: col("final_norm_g", k))

            v.memset(apad[:, :, 0:CK - 1], 0.0)
            v.memset(cpad[:, :, 0:2], 0.0)
            link(v.memset(upad[:, :, 0:2], 0.0), "pads")
            normed("nm", hT, lambda k: col("g_mix_2", k))
            v.wait_ge(S("taken_A"), taken_by("A", BLOCK_AT[("z", 7)]))
            link(v.tensor_tensor(apad[:, :, CK - 1:], apad[:, :, CK - 1:], agate[:, :, :], ALU.mult))
            for tap in range(CK):
                for b in range(CC):
                    wcol = col("conv_a_w_2", tap * CC + b)
                    if tap == 0:
                        ins = v.tensor_scalar(acc[:, b, :], apad[:, b, 0:T], wcol, col("conv_a_b_2", b), ALU.mult, ALU.add)
                    else:
                        ins = stt(acc[:, b, :], apad[:, b, tap:tap + T], wcol, acc[:, b, :], ALU.mult, ALU.add)
                link(ins, "conv_a" if tap == CK - 1 else "vec_step")
            v.wait_ge(S("taken_A"), taken_by("A", BLOCK_AT[("z", 19)]))
            link(v.tensor_tensor(cpad[:, :, 2:], cpad[:, :, 2:], scc[:, :, :], ALU.mult))
            for tap in range(3):
                for b in range(CC):
                    wcol = col("conv_b_w_2", tap * CC + b)
                    if tap == 0:
                        ins = v.tensor_scalar(sT[:, b, :], cpad[:, b, 0:T], wcol, None, ALU.mult)
                    else:
                        ins = stt(sT[:, b, :], cpad[:, b, tap:tap + T], wcol, sT[:, b, :], ALU.mult, ALU.add)
                link(ins)
            link(v.tensor_tensor(sT[:, :, :], sT[:, :, :], scb[:, :, :], ALU.mult), "conv_b")
            v.wait_ge(S("ln_sum"), 1)
            link(v.tensor_scalar(stat[:, 1, :], BK[4][:, 0:T], 1.0 / 512, None, ALU.mult))
            for b in range(CC):
                ins = v.tensor_tensor(acc[:, b, :], acc[:, b, :], stat[:, 1, :], ALU.subtract)
            link(ins, "ln_mean")
            v.wait_ge(S("ln_std"), 1)
            link(v.reciprocal(stat[:, 1, :], stat[:, 0, :]))
            for b in range(CC):
                ins = stt(acc[:, b, :], acc[:, b, :], col("ln_a_g_2", b), stat[:, 1, :])
            link(ins, "ln_norm")
            v.wait_ge(S("taken_A"), taken_by("A", BLOCK_AT[("z", 35)]))
            for b in range(8):
                link(v.tensor_tensor(comb2[:, b, :], arrived(("ya", b))[:, 0:T], zg[:, b, :], ALU.mult), "taken_V")
            for b in range(8):
                link(v.tensor_tensor(zg[:, 8 + b, :], arrived(("yb", b))[:, 0:T], zg[:, 8 + b, :], ALU.mult), "taken_V")
            link(v.tensor_tensor(comb2[:, :, :], comb2[:, :, :], zg[:, 8:16, :], ALU.add), "comb2")

            def residual(key, sem):
                for b in range(8):
                    link(v.tensor_tensor(xT[:, b, :], arrived((key, b))[:, 0:T], xT[:, b, :], ALU.add), "taken_V")
                v.sem_inc(S(sem), 1)

            residual("o", "x3")
            normed("nff", hT, lambda k: col("g_ffn_2", k))
            for b in range(FB):
                v.wait_ge(S("taken_A"), taken_by("A", BLOCK_AT[("up", b)]))
                for tap in range(3):
                    wcol = col("conv_f_w_2", tap * FB + b)
                    if tap == 0:
                        ins = v.tensor_scalar(fT[:, b, :], upad[:, b, 0:T], wcol, None, ALU.mult)
                    else:
                        ins = stt(fT[:, b, :], upad[:, b, tap:tap + T], wcol, fT[:, b, :], ALU.mult, ALU.add)
                    link(ins, "conv_f" if tap == 2 else "vec_step")
            for b in range(FB):
                v.wait_ge(S("ffn_gelu"), b + 1)
                link(v.tensor_tensor(fT[:, b, :], arrived(("up", FB + b))[:, 0:T], fT[:, b, :], ALU.mult), "taken_V")
            v.sem_inc(S("ffn"), 1)
            residual("down", "x4")
            normed("np", hT, lambda k: col("g_ple_2", k))
            for b in range(8):
                bank = arrived(("pl", b))
                if b == 0:
                    v.wait_ge(S("taken_A"), taken_by("A", BLOCK_AT[("pg", 7)]))
                link(v.tensor_tensor(pgT[:, b, :], bank[:, 0:T], pgT[:, b, :], ALU.mult), "taken_V")
                ins = v.tensor_tensor(xT[:, b, :], xT[:, b, :], pgT[:, b, :], ALU.add)
                link(ins, "x5" if b == 7 else "vec_step")
            normed("nl", hT, lambda k: col("g_final_2", k))


def kernel(**inputs):
    import numpy as np
    import concourse.bacc as bacc
    from concourse.bass_utils import run_bass_kernel_spmd

    nc = bacc.Bacc("TRN2", target_bir_lowering=False, num_devices=1)
    arrays, w = {}, {}
    for name in INPUTS:
        a = np.ascontiguousarray(inputs[name])
        arrays["in_" + name] = a
        w[name] = nc.dram_tensor("in_" + name, a.shape, mybir.dt.from_np(a.dtype), kind="ExternalInput").ap()
    out = nc.dram_tensor("out_0", (1, T, D), F32, kind="ExternalOutput").ap()
    two_blocks(nc, w, out)
    r = run_bass_kernel_spmd(nc, [arrays], core_ids=[0])
    return r.results[0]["out_0"]
```

```python
from contextlib import ExitStack

import concourse.bass as bass
from concourse import mybir

F32 = mybir.dt.float32
U32 = mybir.dt.uint32
F32R = mybir.dt.float32r
ALU = mybir.AluOpType
ACT = mybir.ActivationFunctionType
X = mybir.AxisListType.X

P = 128
T = 256
NT = T // P
D = 1024
KD = D // P
EPS = 1e-6
SLOTS = 3
SLOT = 8 * 528
BANKS = 4

GH, DK, DV, CH = 4, 128, 256, 64
TAU = 16.0
AH, LAT, IH, TOPK = 8, 256, 8, 64
OUT_OF = -1e30
TAKEN = -3e38
EH, EK, NKEY = 8, 16, 128
QUARTERS = 4
PER_Q = EK // QUARTERS
CK, CC = 31, 4
FB = 22

O_GQ, O_GK, O_GV, O_GR, O_LOW, O_DQ, O_KV, O_IQ, O_IK, O_IW, O_ZA, O_ZB = (
    0, 512, 1024, 2048, 3072, 3088, 4112, 4368, 4880, 4944, 4952, 5976)

ROWS = [("b_ada", 0, 0, 48), ("norm1_g", 0, 48, 8), ("gla_b_gate", 0, 56, 4), ("gla_norm_g", 0, 60, 8),
        ("dsa_kv_norm_g", 0, 68, 2), ("norm2_g", 0, 70, 8), ("final_norm_g", 0, 78, 8), ("c", 0, 86, 8),
        ("g_mix_2", 1, 0, 8), ("b_gate_2", 1, 8, 16), ("conv_a_b_2", 1, 24, 4), ("ln_a_g_2", 1, 28, 4),
        ("ln_a_b_2", 1, 32, 4), ("g_ffn_2", 1, 36, 8), ("conv_f_b_2", 1, 44, 22), ("g_ple_2", 1, 66, 8),
        ("g_final_2", 1, 74, 8), ("conv_b_w_2", 1, 82, 12),
        ("conv_a_w_2", 2, 0, 124), ("conv_f_w_2", 3, 0, 66)]
ROW_TILES = [94, 94, 124, 66]
ROWS_0 = sum(t == 0 for _, t, _, _ in ROWS)


def work_table():
    chunks, blocks = [], []

    def chunk(key, name, kt, col, n, k0=0):
        chunks.append((key, name, kt, k0, col, n))

    def block(key, engine, back=0):
        blocks.append((key, engine, len(chunks) - 1 - back))

    def ada(j):
        chunk(("ada", j), "w_ada", KD, 512 * j, 512)
        block(("ada", j), "V")

    for j in range(4):
        ada(j)
    for key, col in (("gq", O_GQ), ("gk", O_GK)):
        chunk((key, 0), "w_in", KD, col, 512)
        for b in range(4):
            block((key, b), "A")
    for j in range(2):
        chunk(("gv", j), "w_in", KD, O_GV + 512 * j, 512)
        for t in range(NT):
            block(("gv", j, t), "A")
    chunk(("low", 0), "w_in", KD, O_LOW, 528)
    block(("low", 0), "A")
    for b in range(4):
        block(("dq", b), "A")
    chunk(("dq", 1), "w_in", KD, O_DQ + 512, 512)
    for b in range(4, 8):
        block(("dq", b), "A")
    chunk(("kv", 0), "w_in", KD, O_KV, 512)
    for b in range(2):
        block(("kv", b), "A")
    for b in range(2):
        block(("iq", b), "A")
    chunk(("iq", 1), "w_in", KD, O_IQ + 256, 328)
    for b in range(2, 4):
        block(("iq", b), "A")
    for b in range(2):
        block(("ik", b), "A")
    for t in range(NT):
        block(("iw", t), "A")
    for j in range(2):
        chunk(("gr", j), "w_in", KD, O_GR + 512 * j, 512)
        for b in range(4):
            block(("gr", 4 * j + b), "A")
    for h in range(AH):
        key, b = ("za", 2 * h) if h < 4 else ("zb", 2 * h - 8)
        if h % 2 == 0:
            chunk((key, b // 4), "w_in", KD, (O_ZA if h < 4 else O_ZB) + 128 * b, 512)
        for i in range(2):
            block((key, b + i), "A", back=h % 2)
        ada(4 + h)
    for key, name in (("ba", "w_branch_a"), ("bb", "w_branch_b"), ("wo", "w_out")):
        for j in range(2):
            chunk((key, j), name, KD, 512 * j, 512)
            for b in range(4):
                block((key, 4 * j + b), "V")
    for j in range(4):
        chunk(("pq", j), "peer_w_q", KD, 512 * j, 512)
        for b in range(4):
            block(("pq", 4 * j + b), "A")
    for j in range(9):
        chunk(("z", j), "w_in_2", KD, 512 * j, 512)
        for b in range(4):
            block(("z", 4 * j + b), "A")
    for key, name in (("yb", "w_b_out_2"), ("ya", "w_a_out_2")):
        chunk((key, 0), name, CC, 0, D)
        for b in range(8):
            block((key, b), "V")
    for j in range(2):
        chunk(("o", j), "w_o_2", KD, 512 * j, 512)
        for b in range(4):
            block(("o", 4 * j + b), "V")
    for j in range(11):
        chunk(("up", j), "w_up_2", KD, 512 * j, 512)
        for b in range(4):
            block(("up", 4 * j + b), "A" if 4 * j + b < FB else "V")
    for j in range(4):
        for half in range(2):
            chunk(("down", j, half), "w_down_2", FB // 2, 256 * j, 256, half * FB // 2)
        for b in range(2):
            block(("down", 2 * j + b), "V")
    for j in range(2):
        chunk(("pg", j), "w_ple_gate_2", KD, 512 * j, 512)
        for b in range(4):
            block(("pg", 4 * j + b), "A")
    chunk(("pl", 0), "w_ple_2", 2, 0, D)
    for b in range(8):
        block(("pl", b), "V")
    return chunks, blocks


CHUNKS, BLOCKS = work_table()
CHUNK_AT = {c[0]: n for n, c in enumerate(CHUNKS)}
BLOCK_AT = {b[0]: n for n, b in enumerate(BLOCKS)}


def taken_by(engine, n):
    return sum(e == engine for _, e, _ in BLOCKS[:n + 1])


def last_product(c):
    return max(n for n, (_, _, at) in enumerate(BLOCKS) if at == c)


PARTED = [n for n, c in enumerate(CHUNKS) if c[0][0] in ("z", "up", "down", "pg")]
PARTED_Z = sum(CHUNKS[n][0][0] == "z" for n in PARTED)


def chunk_of(n):
    return BLOCKS[n][2]


INPUTS = ["x", "c", "w_ada", "b_ada", "norm1_g", "w_in", "gla_w_gate_up", "gla_b_gate", "gla_norm_g",
          "dsa_kv_norm_g", "dsa_w_uk", "dsa_w_uv", "w_branch_a", "w_branch_b", "w_out", "norm2_g",
          "peer_w_q", "peer_sub_keys_1", "peer_sub_keys_2", "peer_u", "peer_v", "final_norm_g", "p_2",
          "g_mix_2", "w_in_2", "b_gate_2", "conv_a_w_2", "conv_a_b_2", "ln_a_g_2", "ln_a_b_2",
          "w_a_out_2", "conv_b_w_2", "w_b_out_2", "w_o_2", "g_ffn_2", "w_up_2", "conv_f_w_2",
          "conv_f_b_2", "w_down_2", "g_ple_2", "w_ple_2", "w_ple_gate_2", "g_final_2"]


def rows_of(ap):
    n = len(ap.shape)
    if n == 1:
        return ap.rearrange("(r p) -> r p", p=P)
    if n == 2:
        return ap.rearrange("a (r p) -> (a r) p", p=P)
    return ap.rearrange("a b (r p) -> (a b r) p", p=P)


def two_blocks(nc, w, out):
    with ExitStack() as ctx:
        made = {}

        def S(name):
            if name not in made:
                made[name] = ctx.enter_context(nc.semaphore(name))
            return made[name]

        def sb(name, shape, dt=F32):
            return ctx.enter_context(nc.sbuf_tensor(name, shape, dt))

        ps = ctx.enter_context(nc.psum_tensor("ps", [P, 8, 512], F32))
        BK = [ps[:, b, :] for b in range(8)]

        ident, ones, epsc = sb("ident", [P, P]), sb("ones", [P, P]), sb("epsc", [P, 1])
        iota16 = sb("iota16", [P, EK])
        negdist = sb("negdist", [P, NT, T])
        vec = sb("vec", [P, 4, P])
        keyT = sb("keyT", [P, 2, P])
        csil = sb("csil", [P, KD])
        adaT = sb("adaT", [P, 48])
        mod = sb("mod", [P, KD])
        xT, sq = sb("xT", [P, KD, T]), sb("sq", [P, KD, T])
        stat = sb("stat", [P, 2, T])
        topu = sb("topu", [P, 2, EK], U32)
        ciu = sb("ciu", [P, 3, EK], U32)
        rowid = sb("rowid", [P, 2, EK], U32)
        SIZE = 32080

        def overlay(*tensors):
            with ExitStack() as over:
                return [over.enter_context(nc.sbuf_tensor(*t)) for t in tensors]

        arena, hT, wring = overlay(("arena", [P, SIZE], F32), ("hT", [P, KD, T], F32),
                                   ("wring", [P, SLOTS, SLOT], F32))
        at = [0]

        def view(*dims):
            n = 1
            for d in dims:
                n *= d
            a = arena[:, at[0]:at[0] + n]
            at[0] += n
            assert at[0] <= SIZE, at[0]
            if len(dims) == 2:
                a = a.rearrange("p (a b) -> p a b", b=dims[1])
            if len(dims) == 3:
                a = a.rearrange("p (a b c) -> p a b c", b=dims[1], c=dims[2])
            if len(dims) == 4:
                a = a.rearrange("p (a b c d) -> p a b c d", b=dims[1], c=dims[2], d=dims[3])
            return a

        def again(start, *dims):
            at[0] = start
            return view(*dims)

        def col(name, i):
            t, r = next((t, r) for n, t, r, _ in ROWS if n == name)
            return vec[:, t, r + i:r + i + 1]

        def cols(name, n):
            t, r = next((t, r) for m, t, r, _ in ROWS if m == name)
            return vec[:, t, r:r + n]

        a_x = at[0]
        xtok = view(NT, D)
        a_qk = at[0]
        gq, gk = view(GH, T), view(GH, T)
        a_gv = at[0]
        gv = view(NT, D)
        low = view(T)
        dqT, kvT, iqT, ikT = view(AH, T), view(2, T), view(4, T), view(2, T)
        iw = view(NT, IH)
        gr, za, zb = view(KD, T), view(KD, T), view(KD, T)
        a_r1 = at[0]
        la, cum, ediff, ework = (view(GH * T) for _ in range(4))
        kendT = view(2 * GH, P)
        attn = view(2 * GH, P)
        gT = view(KD, T)
        wuv = view(AH, 2, P)
        scanmask = view(T)
        decay = view(GH * 4)
        ckv_tok = view(NT, LAT)
        madd = view(NT, T)
        a_score = at[0]
        score, work = view(T), view(T)
        m8 = view(8)
        rel, pr = view(2, T), view(2, T)
        pT = view(3, P)
        qlat, olat = view(2, T), view(2, T)
        sm = view(8)
        vrows = again(a_r1, 4, P)
        keyrows = view(2, P)
        wgate = again(a_score, 512)
        oT = again(a_x, KD, T)
        dsaT = again(a_qk, AH, T)
        comb = again(a_gv, KD, T)
        state = again(a_r1, 3, GH, DV)
        ada_sum = view(2, 512)
        ostd = again(a_score, GH * T)
        wuk = sq[:, :, :]

        at[0] = 0
        h2tok = view(NT, D)
        qs = view(4, T)
        s_all = view(NT * EH + 1, 2 * NKEY)
        pacc = view(NT, D)
        diag = view(EK, P)
        urows = view(EK, D)
        cur = view(2 * NKEY)
        cur2 = view(2 * NKEY)
        cand = view(EK, EK)
        cand2 = view(EK, EK)
        oneh = view(EK, EK)
        top = view(2, EK)
        topi = view(2, EK)
        best = view(EK)
        ci = view(2, EK)
        pick = view(2, EK)
        expb = view(EK)
        gst = view(4)
        dots = view(2, EK)
        gel = view(EK)
        amul = view(2, EK)
        by_row = [a.rearrange("p a b -> p (a b)") for a in (wring[:, :, :], sq[:, :, :], hT[:, :, :])]
        slots = [CHUNK_AT[("pq", q + 1)] % SLOTS for q in range(SLOTS)]
        vrows_e = [by_row[0][:, slot * SLOT + j * D:slot * SLOT + (j + 1) * D] for slot in slots for j in range(PER_Q)]
        vrows_e += [a[:, j * D:(j + 1) * D] for a in by_row[1:] for j in range(KD * T // D)]

        at[0] = 0
        ptok = view(NT, 256)
        pleT = view(2, T)
        a_branch = at[0]
        apad = view(CC, CK - 1 + T)
        agate = view(CC, T)
        acc = view(CC, T)
        scb, scc = view(CC, T), view(CC, T)
        cpad = view(CC, 2 + T)
        sT = view(CC, T)
        zg = view(16, T)
        comb2 = view(KD, T)
        a_ffn = at[0]
        upad = view(FB, 2 + T)
        at[0] = -(-at[0] // 8) * 8
        fT = view(FB, T)
        pgT = view(KD, T)
        a_hi = -(-at[0] // 8) * 8
        otok = again(a_hi - KD * T - FB * T, NT, D)
        W = KD * 512
        a_f = -(-(a_ffn + FB * (2 + T)) // 8) * 8
        _, w_hi_z, _, h_hi, _, h_lo, w_lo = overlay(
            ("to_z", [P, a_ffn], F32), ("w_hi_z", [P, SLOTS, W], F32R),
            ("to_h", [P, a_hi - a_ffn - SLOTS * W], F32), ("h_hi", [P, KD, T], F32R),
            ("to_end", [P, SIZE - a_hi - KD * T], F32), ("h_lo", [P, KD, T], F32R),
            ("w_lo", [P, SLOTS, SLOT], F32R))
        _, w_hi_up, _, f_hi = overlay(("to_up", [P, a_branch], F32), ("w_hi_up", [P, SLOTS, W], F32R),
                                      ("to_f_hi", [P, a_ffn - a_branch - SLOTS * W], F32),
                                      ("f_hi", [P, FB, T], F32R))
        _, f_lo = overlay(("to_f", [P, a_f], F32), ("f_lo", [P, FB, T], F32R))

        block = ctx.enter_context(nc.Block())

        def parts(c):
            name, r = CHUNKS[c][0][0], PARTED.index(c)
            n = CHUNKS[c][2] * CHUNKS[c][5]
            hi, slot = (w_hi_z, r % SLOTS) if name == "z" else (w_hi_up, (r - PARTED_Z) % SLOTS)
            return wring[:, c % SLOTS, 0:n], hi[:, slot, 0:n], w_lo[:, c % SLOTS, 0:n]

        def by_block(a, n=512):
            return a.rearrange("p (k n) -> p k n", n=n)

        @block.sync
        def _(sp):
            for name, t, r, k in ROWS[:ROWS_0]:
                sp.dma_start(vrows[r:r + k, t, :], rows_of(w[name])).then_inc(S("rows_in"), 16)

            def load(n):
                key, name, kt, k0, c0, nn = CHUNKS[n]
                if n >= SLOTS:
                    before = CHUNKS[n - SLOTS][0]
                    if before[0] == "down" and before[2] == 0:
                        sp.wait_ge(S("down_half"), before[1] + 1)
                    else:
                        sp.wait_ge(S("product"), last_product(n - SLOTS) + 1)
                if key == ("z", 0):
                    sp.wait_ge(S("v_used"), NT * EH * EK)
                dst = wring[:, n % SLOTS, 0:kt * nn].rearrange("p (k n) -> p k n", n=nn)
                src = w[name][0].rearrange("(k p) n -> p k n", p=P)[:, k0:k0 + kt, c0:c0 + nn]
                sp.dma_start(dst, src).then_inc(S(f"chunk{n % SLOTS}"), 16)

            for n in range(len(CHUNKS)):
                load(n)
                if n == CHUNK_AT[("ada", 0)]:
                    sp.dma_start(xtok[:, :, :], w["x"][0].rearrange("(t p) d -> p t d", p=P)).then_inc(S("x_in"), 16)
                if n == CHUNK_AT[("gq", 0)]:
                    sp.wait_ge(S("n1_ss"), KD)
                    sp.dma_start(wuk.rearrange("p a b -> p (a b)").rearrange("p (h c) -> p h c", c=LAT),
                                 w["dsa_w_uk"][0].rearrange("h d c -> d h c")).then_inc(S("wuk_in"), 16)
                    sp.dma_start(wuv, w["dsa_w_uv"][0].rearrange("h (b c) d -> c h b d", c=P)).then_inc(S("wuv_in"), 16)
                if n == CHUNK_AT[("z", 2)]:
                    sp.dma_start(ptok[:, :, :], w["p_2"][0, 0].rearrange("(t p) d -> p t d", p=P)).then_inc(S("p_in"), 16)
            for t in range(NT):
                sp.wait_ge(S("out_cp"), 3 + t)
                sp.dma_start(out[0, t * P:(t + 1) * P, :], otok[:, t, :]).then_inc(S("stored"), 16)
            sp.wait_ge(S("stored"), 16 * NT)

        @block.gpsimd
        def _(pool):
            n_chain = [0]

            def link(ins, name=None):
                if name is None:
                    n_chain[0] += 1
                    ins.then_inc(S("pool_step"), 1)
                    pool.wait_ge(S("pool_step"), n_chain[0])
                else:
                    ins.then_inc(S(name), 1)

            link(pool.memset(ident[:, :], 0.0))
            link(pool.affine_select(out=ident[:, :], in_=ident[:, :], compare_op=ALU.not_equal, fill=1.0, base=0,
                                    pattern=[[-1, P]], channel_multiplier=1), "ident")
            pool.memset(ones[:, :], 1.0)
            link(pool.memset(epsc[:, :], EPS), "ones")
            link(pool.memset(scanmask, 1.0))
            link(pool.memset(scanmask.rearrange("p (n c) -> p n c", c=CH)[:, :, 0:1], 0.0))
            for t in range(NT):
                pool.iota(negdist[:, t, :], [[1, T]], base=-t * P, channel_multiplier=-1,
                          allow_small_or_imprecise_dtypes=True)
            link(pool.iota(iota16[:, :], [[1, EK]], base=0, channel_multiplier=0, allow_small_or_imprecise_dtypes=True))
            link(pool.memset(ikT[64:128, 0, :], 0.0))
            link(pool.memset(ikT[0:64, 1, :], 0.0))
            link(pool.memset(attn[:, :, :], 0.0), "pool_consts")

            pool.wait_ge(S("n1_std"), 1)
            for k in range(KD):
                pool.tensor_tensor(out=hT[:, k, :], in0=xT[:, k, :], in1=stat[:, 1, :], op=ALU.mult).then_inc(S("n1_x"), 1)

            for t in range(NT):
                nk = P * (t + 1)
                pool.wait_ge(S("index_sum"), IH * (t + 1))
                link(pool.affine_select(out=work[:, 0:nk], in_=score[:, 0:nk], compare_op=ALU.is_ge, fill=OUT_OF,
                                        base=t * P, pattern=[[-1, nk]], channel_multiplier=1), "causal")
                pool.wait_ge(S("picked"), t + 1)
                link(pool.affine_select(out=madd[:, t, 0:nk], in_=madd[:, t, 0:nk], compare_op=ALU.is_ge, fill=OUT_OF,
                                        base=t * P, pattern=[[-1, nk]], channel_multiplier=1), "madd_ready")
            pool.wait_ge(S("attn_cp"), 1)
            link(pool.affine_select(out=attn[:, :, :], in_=attn[:, :, :], compare_op=ALU.is_ge, fill=0.0, base=0,
                                    pattern=[[0, 2 * GH], [1, P]], channel_multiplier=-1), "attn_ready")

            pool.wait_ge(S("o_normed"), 1)
            pool.wait_ge(S("taken_A"), taken_by("A", BLOCK_AT[("gr", 7)]))
            link(pool.tensor_tensor(out=gT[:, :, :], in0=oT[:, :, :], in1=gr[:, :, :], op=ALU.mult), "gla_out")

            U, Vx = w["peer_u"][0], w["peer_v"][0]

            def gather(g, j, even, table, dst, sem):
                pool.indirect_dma_start(out=dst, out_offset=None, in_=table,
                                        in_offset=bass.IndirectOffsetOnAxis(ap=rowid[:, even, j:j + 1], axis=0)
                                        ).then_inc(sem, 16)

            def head(g, even, first):
                pool.wait_ge(S("rows_ready"), g + 1)
                pool.sem_inc(S("tick"), 1)
                for q in range(QUARTERS):
                    if not first:
                        pool.wait_ge(S("dot"), (g - 1) * EK + PER_Q * (q + 1))
                        pool.sem_inc(S("tick"), 1)
                    for j in range(PER_Q * q, PER_Q * (q + 1)):
                        gather(g, j, even, U, urows[:, j, :], S(f"u_in{q}"))
                for q in range(QUARTERS):
                    if first:
                        pool.wait_ge(S("product"), BLOCK_AT[("pq", min(4 * q + 7, 15))] + 1)
                    if not first:
                        pool.wait_ge(S("v_used"), (g - 1) * EK + PER_Q * (q + 1))
                        pool.sem_inc(S("tick"), 1)
                    for j in range(PER_Q * q, PER_Q * (q + 1)):
                        gather(g, j, even, Vx, vrows_e[j], S(f"v_in{q}"))

            head(0, 0, True)
            with pool.Fori(1, EH - 1, 2) as g:
                head(g, 1, False)
                head(g + 1, 0, False)
            head(EH - 1, 1, False)
            head(EH, 0, False)
            with pool.Fori(EH + 1, 2 * EH - 1, 2) as g:
                head(g, 1, False)
                head(g + 1, 0, False)
            head(2 * EH - 1, 1, False)

            def rest(r):
                whole, hi, lo = parts(PARTED[r])
                pool.wait_ge(S("w_hi"), r + 1)
                pool.tensor_tensor(out=lo, in0=whole, in1=hi.bitcast(F32), op=ALU.subtract).then_inc(S("w_lo"), 1)

            def rest_of_h(n):
                for k in range(KD):
                    pool.wait_ge(S("h_hi"), KD * n + k + 1)
                    pool.tensor_tensor(out=h_lo[:, k, :], in0=hT[:, k, :], in1=h_hi[:, k, :].bitcast(F32),
                                       op=ALU.subtract).then_inc(S("h_lo"), 1)

            for r, c in enumerate(PARTED):
                rest(r)
                if CHUNKS[c][0] in (("z", 0), ("up", 0), ("pg", 0)):
                    rest_of_h(("z", "up", "pg").index(CHUNKS[c][0][0]))

        @block.tensor
        def _(pe):
            done = [0]

            def begin(key):
                n = BLOCK_AT[key]
                assert n == done[0], (key, n, done[0])
                done[0] += 1
                c = chunk_of(n)
                if key[0] == "down":
                    pass
                elif c in PARTED:
                    pe.wait_ge(S("w_lo"), PARTED.index(c) + 1)
                elif key[0] != "ada" and (n == 0 or chunk_of(n - 1) != c):
                    pe.wait_ge(S(f"chunk{c % SLOTS}"), 16 * (c // SLOTS + 1))
                if n >= BANKS:
                    e = BLOCKS[n - BANKS][1]
                    pe.wait_ge(S("taken_" + e), taken_by(e, n - BANKS))
                _, _, kt, _, _, nn = CHUNKS[c]
                return BK[n % BANKS], wring[:, c % SLOTS, 0:kt * nn].rearrange("p (k n) -> p k n", n=nn)

            def product(key, rhs, c0, m=P, kt=KD, ready=None):
                bank, wt = begin(key)
                for k in range(kt):
                    if ready:
                        pe.wait_ge(S(ready), k + 1)
                    mm = pe.matmul(bank[0:m, 0:T], wt[:, k, c0:c0 + m], rhs[:, k, :], start=k == 0, stop=k == kt - 1)
                mm.then_inc(S("product"), 1)

            def product_parted(key, c0, first=0):
                bank, _ = begin(key)
                hi, lo = (by_block(a) for a in parts(chunk_of(BLOCK_AT[key]))[1:])
                for k in range(KD):
                    if first:
                        pe.wait_ge(S("h_hi"), KD * (first - 1) + k + 1)
                    pe.matmul(bank[:, 0:T], hi[:, k, c0:c0 + P], h_hi[:, k, :], start=k == 0, stop=False)
                    pe.matmul(bank[:, 0:T], lo[:, k, c0:c0 + P], h_hi[:, k, :], start=False, stop=False)
                    if first:
                        pe.wait_ge(S("h_lo"), KD * (first - 1) + k + 1)
                    mm = pe.matmul(bank[:, 0:T], hi[:, k, c0:c0 + P], h_lo[:, k, :], start=False, stop=k == KD - 1)
                mm.then_inc(S("product"), 1)

            def products(name, rhs, c0, kt=KD, ready=None, squares=None):
                for b in range(8):
                    product((name, b), rhs, c0(b), kt=kt, ready=ready if b == 0 else None)
                    if squares and b >= 2:
                        sum_block(squares, b - 2)
                if squares:
                    sum_block(squares, 6)
                    sum_block(squares, 7)

            def product_tok(key, t, c0, n):
                bank, wt = begin(key)
                for k in range(KD):
                    mm = pe.matmul(bank[:, 0:n], hT[:, k, t * P:(t + 1) * P], wt[:, k, c0:c0 + n],
                                   start=k == 0, stop=k == KD - 1)
                mm.then_inc(S("product"), 1)

            def ada(j):
                bank, _ = begin(("ada", j))
                pe.wait_ge(S("ada_sum"), j + 1)
                for b in range(4):
                    mm = pe.matmul(bank[:, b:b + 1], ada_sum[:, j % 2, b * P:(b + 1) * P], ones[:, 0:1],
                                   start=True, stop=True)
                mm.then_inc(S("product"), 1)

            def sum_block(tag, k):
                pe.wait_ge(S(tag + "_sq"), k + 1)
                pe.matmul(BK[4][:, 0:T], ones[:, :], sq[:, k, :], start=k == 0, stop=k == KD - 1,
                          skip_group_check=True).then_inc(S(tag + "_ss"), 1)

            def sum_all(ready, summed, n, src, bank):
                pe.wait_ge(S(ready), 1)
                for k in range(n):
                    mm = pe.matmul(BK[bank][:, 0:T], ones[:, :], src[:, k, :], start=k == 0, stop=k == n - 1)
                mm.then_inc(S(summed), 1)

            def turn_vectors(tiles, bank, sem):
                for i in tiles:
                    n = ROW_TILES[i]
                    mm = pe.transpose(BK[bank][:, i * P:i * P + n], vrows[0:n, i, :], ident[0:n, 0:n])
                mm.then_inc(S(sem), 1)

            pe.wait_ge(S("ident"), 1)
            pe.wait_ge(S("rows_in"), 16 * ROWS_0)
            turn_vectors(range(1), 5, "vec_mm")
            pe.wait_ge(S("x_in"), 16)
            pe.wait_ge(S("vec"), 1)
            for b in range(4):
                for k in (2 * b, 2 * b + 1):
                    for t in range(NT):
                        mm = pe.transpose(BK[4 + b][:, (k % 2) * T + t * P:(k % 2) * T + (t + 1) * P],
                                          xtok[:, t, k * P:(k + 1) * P], ident[:, :])
                mm.then_inc(S("x_mm"), 1)
            pe.wait_ge(S("ones"), 1)
            ada(0)
            pe.wait_ge(S("xT"), 4)
            for k in range(KD):
                sum_block("n1", k)
            for j in range(1, 4):
                ada(j)

            for key in ("gq", "gk"):
                for b in range(4):
                    product((key, b), hT, b * P, ready="n1_h" if (key, b) == ("gq", 0) else None)
            pe.wait_ge(S("rows_late_in"), 16 * (len(ROWS) - ROWS_0))
            turn_vectors(range(1, 4), 6, "vec_late_mm")
            pe.wait_ge(S("keys_in"), 32)
            for i in range(2):
                mm = pe.transpose(BK[7][:, i * P:(i + 1) * P], keyrows[:, i, :], ident[:, :])
            mm.then_inc(S("vec_late_mm"), 1)
            for j in range(2):
                for t in range(NT):
                    product_tok(("gv", j, t), t, 0, 512)
            product(("low", 0), hT, 0, m=16)
            for b in range(8):
                product(("dq", b), hT, 16 + b * P if b < 4 else (b - 4) * P)
            for b in range(2):
                product(("kv", b), hT, b * P)
            for b in range(4):
                product(("iq", b), hT, 256 + b * P if b < 2 else (b - 2) * P)
            product(("ik", 0), hT, 256, m=64)
            product(("ik", 1), hT, 192)
            for t in range(NT):
                product_tok(("iw", t), t, 320, IH)

            pe.wait_ge(S("taken_A"), taken_by("A", BLOCK_AT[("low", 0)]))
            pe.wait_ge(S("wgate_in"), 16)
            pe.wait_ge(S("keyT"), 1)
            for h in range(GH):
                mm = pe.matmul(BK[6 + h // 2][:, (h % 2) * T:(h % 2 + 1) * T], wgate[0:16, h * P:(h + 1) * P],
                               low[0:16, :], start=True, stop=True)
            mm.then_inc(S("gate_mm"), 1)
            sum_all("kv_sq", "kv_ss", 2, rel, 4)
            for b in range(4):
                product(("gr", b), hT, b * P)
            pe.wait_ge(S("kv_h"), 1)
            for t in range(NT):
                for b in range(2):
                    mm = pe.transpose(BK[5][:, t * LAT + b * P:t * LAT + (b + 1) * P], kvT[:, b, t * P:(t + 1) * P],
                                      ident[:, :])
            mm.then_inc(S("ckv_mm"), 1)

            pe.wait_ge(S("pool_consts"), 1)
            pe.wait_ge(S("taken_A"), taken_by("A", BLOCK_AT[("ik", 1)]))
            for t in range(NT):
                for h in range(IH):
                    i = t * IH + h
                    if i == 1:
                        pe.wait_ge(S("ckv_tok"), 1)
                    if i >= 2:
                        pe.wait_ge(S("rel"), i - 1)
                    pe.matmul(BK[4 + i % 2][:, 0:P * (t + 1)], iqT[:, h // 2, t * P:(t + 1) * P],
                              ikT[:, h % 2, 0:P * (t + 1)], start=True, stop=True).then_inc(S("index_mm"), 1)
                if t == 0:
                    pe.wait_ge(S("gla_in"), 1)
                    for i in range(2):
                        for j in range(4 * i, 4 * i + 4):
                            mm = pe.transpose(BK[6 + i][:, (j % 4) * P:(j % 4 + 1) * P],
                                              ediff[:, j * P:(j + 1) * P], ident[:, :])
                        mm.then_inc(S("kend_mm"), 1)
                    for b in range(4, 6):
                        product(("gr", b), hT, (b - 4) * P)

            for i in range(2):
                pe.wait_ge(S("kendT"), i + 1)
                for j in range(4 * i, 4 * i + 4):
                    h, t = j // 2, j % 2
                    mm = pe.matmul(BK[6 + i][:, (j % 4) * P:(j % 4 + 1) * P], gk[:, h, t * P:(t + 1) * P],
                                   gq[:, h, t * P:(t + 1) * P], start=True, stop=True)
                mm.then_inc(S("attn_mm"), 1)
            for b in range(6, 8):
                product(("gr", b), hT, (b - 4) * P)
            pe.wait_ge(S("attn_cp"), 1)
            for n in range(3):
                t, half = n // 2, slice((n % 2) * CH, (n % 2 + 1) * CH)
                if n:
                    pe.wait_ge(S("state"), n)
                for h in range(GH):
                    mm = pe.matmul(BK[6 + h // 2][:, (h % 2) * DV:(h % 2 + 1) * DV], kendT[half, 2 * h + t, :],
                                   gv[half, t, h * DV:(h + 1) * DV], start=True, stop=True)
                mm.then_inc(S("update_mm"), 1)
            pe.wait_ge(S("state"), 3)
            pe.wait_ge(S("attn_ready"), 1)
            for h in range(GH):
                if h >= 2:
                    pe.wait_ge(S("o_cp"), h - 1)
                for b in range(2):
                    for t in range(NT):
                        o = BK[6 + h % 2][:, b * T + t * P:b * T + (t + 1) * P]
                        mm = pe.matmul(o, gv[:, t, h * DV + b * P:h * DV + (b + 1) * P], attn[:, 2 * h + t, :],
                                       start=True, stop=False, skip_group_check=True)
                        for n in (2 * t, 2 * t + 1):
                            if n:
                                c = (n % 2) * CH
                                mm = pe.matmul(o[:, c:c + CH], state[:, n - 1, h, b * P:(b + 1) * P],
                                               gq[:, h, t * P + c:t * P + c + CH], start=False, stop=n % 2 == 1,
                                               skip_group_check=True)
                mm.then_inc(S("o_mm"), 1)
            pe.wait_ge(S("o_sq"), GH)
            for h in range(GH):
                for b in range(2):
                    mm = pe.matmul(BK[6 + h // 2][:, (h % 2) * T:(h % 2 + 1) * T], ones[:, :], gT[:, 2 * h + b, :],
                                   start=b == 0, stop=b == 1)
            mm.then_inc(S("o_ss"), 1)

            pe.wait_ge(S("wuk_in"), 16)
            pe.wait_ge(S("wuv_in"), 16)
            pe.wait_ge(S("rel"), NT * IH)
            pe.wait_ge(S("o_std"), 1)
            wuk_h = wuk.rearrange("p a b -> p (a b)").rearrange("p (h c) -> p h c", c=LAT)
            for h in range(AH):
                if h:
                    pe.wait_ge(S("dsa_cp"), h)
                for b in range(2):
                    mm = pe.matmul(BK[4][:, b * T:(b + 1) * T], wuk_h[:, h, b * P:(b + 1) * P], dqT[:, h, :],
                                   start=True, stop=True)
                mm.then_inc(S("qlat_mm"), 1)
                z, b0 = "za" if h < 4 else "zb", 2 * h % 8
                product((z, b0), hT, (b0 % 4) * P)
                pe.wait_ge(S("qlat"), h + 1)
                for t in range(NT):
                    for b in range(2):
                        mm = pe.matmul(BK[5][:, t * P:t * P + P * (t + 1)], qlat[:, b, t * P:(t + 1) * P],
                                       kvT[:, b, 0:P * (t + 1)], start=b == 0, stop=b == 1)
                mm.then_inc(S("logit_mm"), 1)
                product((z, b0 + 1), hT, (b0 % 4 + 1) * P)
                pe.wait_ge(S("p_ready"), h + 1)
                for i, (t, kt) in enumerate(((0, 0), (1, 0), (1, 1))):
                    mm = pe.transpose(BK[6][:, i * P:(i + 1) * P], pr[:, t, kt * P:(kt + 1) * P], ident[:, :])
                mm.then_inc(S("pT_mm"), 1)
                pe.wait_ge(S("pT"), h + 1)
                for b in range(2):
                    for t in range(NT):
                        for kt in range(t + 1):
                            mm = pe.matmul(BK[7][:, b * T + t * P:b * T + (t + 1) * P],
                                           ckv_tok[:, kt, b * P:(b + 1) * P], pT[:, t + kt, :],
                                           start=kt == 0, stop=kt == t)
                mm.then_inc(S("olat_mm"), 1)
                ada(4 + h)
                pe.wait_ge(S("olat"), h + 1)
                for b in range(2):
                    mm = pe.matmul(BK[4][:, 0:T], wuv[:, h, b, :], olat[:, b, :], start=b == 0, stop=b == 1)
                mm.then_inc(S("dsa_mm"), 1)

            pe.wait_ge(S("gla_out"), 1)
            products("ba", gT, lambda b: (b % 4) * P)
            pe.wait_ge(S("dsa_cp"), AH)
            products("bb", dsaT, lambda b: (b % 4) * P)
            products("wo", comb, lambda b: (b % 4) * P, ready="comb", squares="n2")

            def head_scores(h):
                if h >= 4:
                    pe.wait_ge(S("scores"), h - 3)
                pe.wait_ge(S("taken_A"), taken_by("A", BLOCK_AT[("pq", 2 * h + 1)]))
                for half in range(2):
                    for t in range(NT):
                        mm = pe.matmul(BK[4 + h % 4][:, (2 * t + half) * P:(2 * t + half + 1) * P],
                                       qs[:, (2 * h + half) % 4, t * P:(t + 1) * P], keyT[:, half, :],
                                       start=True, stop=True)
                mm.then_inc(S("score_mm"), 1)

            for b in range(16):
                product(("pq", b), hT, (b % 4) * P, ready="n2_h" if b == 0 else None)
                if b == 1:
                    for i in range(4):
                        for k in range(4 * (i % 2), 4 * (i % 2) + 4):
                            mm = pe.transpose(BK[4 + i][:, (k % 4) * P:(k % 4 + 1) * P],
                                              hT[:, k, (i // 2) * P:(i // 2 + 1) * P], ident[:, :])
                        mm.then_inc(S("h2_mm"), 1)
                    pe.wait_ge(S("h2tok"), 4)
                if b % 2 and b >= 3:
                    head_scores((b - 3) // 2)
            head_scores(7)

            def head(g, even, first):
                if not first:
                    pe.wait_ge(S("head_added"), g)
                for q in range(QUARTERS):
                    pe.wait_ge(S(f"v_in{q}"), 16 * PER_Q * (g + 1))
                    for j in range(PER_Q * q, PER_Q * (q + 1)):
                        if j % PER_Q == 0:
                            pe.wait_ge(S("diag"), g * EK + PER_Q * (q + 1))
                        for b in range(2):
                            mm = pe.matmul(BK[4 + 2 * even + b], diag[:, j, :], vrows_e[j][:, b * 512:(b + 1) * 512],
                                           start=j == 0, stop=j == EK - 1, skip_group_check=True)
                        mm.then_inc(S("v_used"), 1)

            pe.wait_ge(S("scores"), EH)
            head(0, 0, True)
            with pe.Fori(1, EH - 1, 2) as g:
                head(g, 1, False)
                head(g + 1, 0, False)
            head(EH - 1, 1, False)
            head(EH, 0, False)
            with pe.Fori(EH + 1, 2 * EH - 1, 2) as g:
                head(g, 1, False)
                head(g + 1, 0, False)
            head(2 * EH - 1, 1, False)
            pe.wait_ge(S("head_added"), NT * EH + 1)
            for b in range(4):
                for k in (2 * b, 2 * b + 1):
                    for t in range(NT):
                        mm = pe.transpose(BK[4 + b][:, (k % 2) * T + t * P:(k % 2) * T + (t + 1) * P],
                                          pacc[:, t, k * P:(k + 1) * P], ident[:, :])
                mm.then_inc(S("expert_mm"), 1)

            pe.wait_ge(S("expert_x"), KD)
            for tag in ("nf1", "nm"):
                for k in range(KD):
                    sum_block(tag, k)
            for b in range(36):
                product_parted(("z", b), (b % 4) * P, first=1 if b == 0 else 0)
                if b == 30:
                    sum_all("conv_a", "ln_sum", CC, acc, 4)
                if b == 33:
                    sum_all("ln_sq", "ln_ss", CC, sq, 5)
                if b == 19:
                    pe.wait_ge(S("p_in"), 16)
                    for k in range(2):
                        for t in range(NT):
                            mm = pe.transpose(BK[7][:, k * T + t * P:k * T + (t + 1) * P],
                                              ptok[:, t, k * P:(k + 1) * P], ident[:, :])
                    mm.then_inc(S("ple_mm"), 1)

            pe.wait_ge(S("conv_b"), 1)
            products("yb", sT, lambda b: b * P, kt=CC)
            products("ya", acc, lambda b: b * P, kt=CC, ready="branch_a")
            products("o", comb2, lambda b: (b % 4) * P, ready="comb2", squares="nff")

            for b in range(2 * FB):
                product_parted(("up", b), (b % 4) * P, first=2 if b == 0 else 0)
            for j in range(4):
                outs = [begin(("down", 2 * j + b))[0] for b in range(2)]
                for half in range(2):
                    c = CHUNK_AT[("down", j, half)]
                    pe.wait_ge(S("w_lo"), PARTED.index(c) + 1)
                    hi, lo = (by_block(a, 256) for a in parts(c)[1:])
                    for b in range(2):
                        o, cs = outs[b][:, 0:T], slice(b * P, (b + 1) * P)
                        for k in range(FB // 2):
                            f = half * FB // 2 + k
                            if j == 0 and b == 0:
                                pe.wait_ge(S("f_lo"), f + 1)
                            pe.matmul(o, hi[:, k, cs], f_hi[:, f, :], start=f == 0, stop=False, skip_group_check=True)
                            pe.matmul(o, lo[:, k, cs], f_hi[:, f, :], start=False, stop=False, skip_group_check=True)
                            mm = pe.matmul(o, hi[:, k, cs], f_lo[:, f, :], start=False, stop=f == FB - 1,
                                           skip_group_check=True)
                        if half:
                            mm.then_inc(S("product"), 1)
                    if half == 0:
                        mm.then_inc(S("down_half"), 1)
                if j:
                    sum_block("np", 2 * j - 2)
                    sum_block("np", 2 * j - 1)
            sum_block("np", 6)
            sum_block("np", 7)

            for b in range(8):
                product_parted(("pg", b), (b % 4) * P, first=3 if b == 0 else 0)
            pe.wait_ge(S("pleT"), 1)
            products("pl", pleT, lambda b: b * P, kt=2, squares="nl")
            for i in range(2):
                for t in range(NT):
                    for k in range(4 * i, 4 * i + 4):
                        if t == 0:
                            pe.wait_ge(S("nl_h"), k + 1)
                        if k == 0 and t == 0:
                            pe.wait_ge(S("nl_std"), 1)
                        mm = pe.transpose(BK[4 + 2 * t + i][:, (k % 4) * P:(k % 4 + 1) * P],
                                          hT[:, k, t * P:(t + 1) * P], ident[:, :])
                    mm.then_inc(S("out_mm"), 1)

        @block.scalar
        def _(act):
            n_of = {}

            def link(ins, name="act_step"):
                n_of[name] = n_of.get(name, 0) + 1
                ins.then_inc(S(name), 1)
                act.wait_ge(S(name), n_of[name])

            taken = [0]

            def take(key, out, func=ACT.Copy, m=slice(0, P), n=T, **kw):
                b = BLOCK_AT[key]
                assert BLOCKS[b][1] == "A" and taken_by("A", b) == taken[0] + 1, key
                taken[0] += 1
                act.wait_ge(S("product"), b + 1)
                act.activation(out, BK[b % BANKS][m, 0:n], func, **kw).then_inc(S("taken_A"), 1)

            def squares(tag, ready, first=0):
                for k in range(KD):
                    square_block(tag, k, ready, first + k + 1)

            def square_block(tag, k, ready, n):
                act.wait_ge(S(ready), n)
                act.activation(sq[:, k, :], xT[:, k, :], ACT.Square).then_inc(S(tag + "_sq"), 1)

            def square_residual(tag, key):
                squares(tag, "taken_V", taken_by("V", BLOCK_AT[(key, 0)]) - 1)

            parted = [0]

            def part():
                c = PARTED[parted[0]]
                parted[0] += 1
                whole, hi, _ = parts(c)
                act.wait_ge(S(f"chunk{c % SLOTS}"), 16 * (c // SLOTS + 1))
                act.activation(hi, whole, ACT.Copy).then_inc(S("w_hi"), 1)

            def part_h(tag):
                for k in range(KD):
                    act.wait_ge(S(tag + "_h"), k + 1)
                    act.activation(h_hi[:, k, :], hT[:, k, :], ACT.Copy).then_inc(S("h_hi"), 1)

            def root(tag, n, bank=4):
                act.wait_ge(S(tag + "_ss"), KD if n == D else 1)
                inverse_root(stat[:, 1, :], BK[bank][:, 0:T], n, tag + "_std")

            def inverse_root(out, sums, n, name):
                link(act.activation(out, sums, ACT.Ln, scale=1.0 / n, bias=epsc[:, 0:1]))
                act.activation(out, out, ACT.Exp, scale=-0.5).then_inc(S(name), 1)

            act.wait_ge(S("vec"), 1)
            act.activation(csil[:, :], cols("c", KD), ACT.Silu).then_inc(S("csil"), 1)
            for name, t, r, k in ROWS[ROWS_0:]:
                act.dma_start(vrows[r:r + k, t, :], rows_of(w[name])).then_inc(S("rows_late_in"), 16)
            act.dma_start(keyrows[:, 0, :], w["peer_sub_keys_1"][0]).then_inc(S("keys_in"), 16)
            act.dma_start(keyrows[:, 1, :], w["peer_sub_keys_2"][0]).then_inc(S("keys_in"), 16)
            act.dma_start(wgate[0:16, :], w["gla_w_gate_up"][0]).then_inc(S("wgate_in"), 16)
            act.wait_ge(S("ones"), 1)
            for k in range(KD):
                square_block("n1", k, "xT", k // 2 + 1)
            root("n1", D)

            for b in range(4):
                take(("gq", b), gq[:, b, :])
            for b in range(4):
                take(("gk", b), gk[:, b, :])
            for j in range(2):
                for t in range(NT):
                    take(("gv", j, t), gv[:, t, j * 512:(j + 1) * 512], n=512)
            take(("low", 0), low[0:16, :], m=slice(0, 16))
            for b in range(8):
                take(("dq", b), dqT[:, b, :])
            for b in range(2):
                take(("kv", b), kvT[:, b, :])
            for b in range(4):
                take(("iq", b), iqT[:, b, :])
                if b == 1:
                    act.wait_ge(S("taken_A"), taken[0])
                    act.activation(rel[:, :, :], kvT[:, :, :], ACT.Square).then_inc(S("kv_sq"), 1)
            take(("ik", 0), ikT[0:64, 0, :], m=slice(0, 64))
            take(("ik", 1), ikT[64:128, 1, :], m=slice(64, 128))
            for t in range(NT):
                take(("iw", t), iw[:, t, :], n=IH, scale=IH ** -0.5)

            act.wait_ge(S("gate_mm"), 1)
            for h in range(GH):
                ins = act.activation(la[:, h * T:(h + 1) * T], BK[6 + h // 2][:, (h % 2) * T:(h % 2 + 1) * T],
                                     ACT.Identity, bias=col("gla_b_gate", h))
            link(ins)
            link(act.activation(cum, la, ACT.Abs))
            link(act.activation(cum, cum, ACT.Exp, scale=-1.0))
            link(act.activation(cum, cum, ACT.Ln, bias=ones[:, 0:1]), "gate_ln")
            root("kv", LAT)
            for b in range(2):
                take(("gr", b), gr[:, b, :], ACT.Silu)
            act.wait_ge(S("gate_sum"), 1)
            act.activation(ework, cum, ACT.Exp, scale=1.0 / TAU)
            act.activation(la, cum, ACT.Exp, scale=-1.0 / TAU)
            act.activation(ediff, ediff, ACT.Exp, scale=1.0 / TAU).then_inc(S("gate_exp"), 1)
            for b in range(2, 4):
                take(("gr", b), gr[:, b, :], ACT.Silu)

            for t in range(NT):
                for h in range(IH):
                    i = t * IH + h
                    act.wait_ge(S("index_mm"), i + 1)
                    if i >= 2:
                        act.wait_ge(S("index_sum"), i - 1)
                    act.activation(rel[:, i % 2, 0:P * (t + 1)], BK[4 + i % 2][:, 0:P * (t + 1)], ACT.Relu,
                                   scale=64 ** -0.5).then_inc(S("rel"), 1)
                if t == 0:
                    for i in range(2):
                        act.wait_ge(S("kend_mm"), i + 1)
                        act.activation(kendT[:, 4 * i:4 * i + 4, :].rearrange("p a b -> p (a b)"), BK[6 + i],
                                       ACT.Copy).then_inc(S("kendT"), 1)
                    for b in range(4, 6):
                        take(("gr", b), gr[:, b, :], ACT.Silu)
            for i in range(2):
                act.wait_ge(S("attn_mm"), i + 1)
                if i == 0:
                    act.wait_ge(S("pool_consts"), 1)
                src = BK[6 + i].rearrange("p (a b) -> p a b", b=P)
                for c in range(2):
                    half = slice(c * CH, (c + 1) * CH)
                    ins = act.activation(attn[half, 4 * i:4 * i + 4, half], src[half, :, half], ACT.Copy)
            ins.then_inc(S("attn_cp"), 1)
            for b in range(6, 8):
                take(("gr", b), gr[:, b, :], ACT.Silu)
            for h in range(GH):
                act.wait_ge(S("o_mm"), h + 1)
                act.activation(oT[:, 2 * h:2 * h + 2, :].rearrange("p a b -> p (a b)"), BK[6 + h % 2],
                               ACT.Copy).then_inc(S("o_cp"), 1)
                act.wait_ge(S("o_cp"), h + 1)
                act.activation(gT[:, 2 * h:2 * h + 2, :], oT[:, 2 * h:2 * h + 2, :], ACT.Square).then_inc(S("o_sq"), 1)
            act.wait_ge(S("o_ss"), 1)
            for i in range(2):
                ins = act.activation(ostd[:, i * 512:(i + 1) * 512], BK[6 + i], ACT.Ln, scale=1.0 / DV,
                                     bias=epsc[:, 0:1])
            link(ins, "o_log")
            act.activation(ostd, ostd, ACT.Exp, scale=-0.5).then_inc(S("o_std"), 1)

            for h in range(AH):
                za_, b0 = (("za", za), ("zb", zb))[h // 4], 2 * h % 8
                act.wait_ge(S("qlat_mm"), h + 1)
                act.activation(qlat.rearrange("p a b -> p (a b)"), BK[4], ACT.Copy).then_inc(S("qlat"), 1)
                if h % 2 == 0:
                    take((za_[0], b0), za_[1][:, b0, :])
                act.wait_ge(S("logits"), h + 1)
                for t in range(NT):
                    ins = act.activation(pr[:, t, 0:P * (t + 1)], pr[:, t, 0:P * (t + 1)], ACT.Exp,
                                         bias=sm[:, 2 + t:3 + t], accum_out=sm[:, 4 + t:5 + t])
                ins.then_inc(S("p_exp"), 1)
                if h % 2:
                    take((za_[0], b0), za_[1][:, b0, :])
                take((za_[0], b0 + 1), za_[1][:, b0 + 1, :])
                act.wait_ge(S("pT_mm"), h + 1)
                act.activation(pT.rearrange("p a b -> p (a b)"), BK[6][:, 0:3 * P], ACT.Copy).then_inc(S("pT"), 1)
                act.wait_ge(S("olat_mm"), h + 1)
                act.activation(olat.rearrange("p a b -> p (a b)"), BK[7], ACT.Copy).then_inc(S("olat"), 1)
            act.wait_ge(S("taken_A"), taken[0])
            act.activation(za[:, :, :], za[:, :, :], ACT.Sigmoid)
            act.activation(zb[:, :, :], zb[:, :, :], ACT.Sigmoid).then_inc(S("gates"), 1)

            def soften(g):
                act.wait_ge(S("best"), g + 1)
                act.sem_inc(S("tick"), 1)
                act.activation(expb, best, ACT.Exp, bias=gst[:, 0:1], accum_out=gst[:, 1:2]).then_inc(S("best_exp"), 1)

            square_residual("n2", "wo")
            root("n2", D)
            for k in range(KD):
                act.wait_ge(S("n2_scaled"), k + 1)
                act.activation(hT[:, k, :], hT[:, k, :], ACT.Identity, bias=adaT[:, 24 + k:25 + k]).then_inc(S("n2_h"), 1)
            for b in range(16):
                if b == 2:
                    for i in range(4):
                        act.wait_ge(S("h2_mm"), i + 1)
                        act.activation(h2tok[:, i // 2, (i % 2) * 512:(i % 2 + 1) * 512], BK[4 + i],
                                       ACT.Copy).then_inc(S("h2tok"), 1)
                if b == 9:
                    soften(0)
                if b >= 4:
                    act.wait_ge(S("score_mm"), b // 2 - 1)
                take(("pq", b), qs[:, b % 4, :])

            def head(g, even, first, last=False):
                act.wait_ge(S("dot"), EK * (g + 1))
                act.sem_inc(S("tick"), 1)
                act.activation(gel, dots[:, even, :], ACT.Gelu).then_inc(S("gelu"), 1)
                act.wait_ge(S("weight"), g + 1)
                act.sem_inc(S("tick"), 1)
                for j in range(EK):
                    if not first and j % PER_Q == 0:
                        act.wait_ge(S("v_used"), (g - 1) * EK + j + PER_Q)
                        act.sem_inc(S("tick"), 1)
                    act.activation(diag[:, j, :], ident[:, :], ACT.Copy,
                                   scale=amul[:, even, j:j + 1]).then_inc(S("diag"), 1)
                if not last:
                    soften(g + 1)

            head(0, 0, True)
            with act.Fori(1, EH - 1, 2) as g:
                head(g, 1, False)
                head(g + 1, 0, False)
            head(EH - 1, 1, False)
            head(EH, 0, False)
            with act.Fori(EH + 1, 2 * EH - 1, 2) as g:
                head(g, 1, False)
                head(g + 1, 0, False)
            head(2 * EH - 1, 1, False, last=True)

            squares("nf1", "expert_x")
            part()
            root("nf1", D)
            squares("nm", "nf1_h")
            part()
            root("nm", D)
            part_h("nm")

            places = [apad[:, b, CK - 1:] for b in range(4)] + [agate[:, b, :] for b in range(4)]
            places += [scb[:, b, :] for b in range(4)] + [scc[:, b, :] for b in range(4)]
            places += [cpad[:, b, 2:] for b in range(4)]
            for b in range(36):
                if b >= 20:
                    take(("z", b), zg[:, b - 20, :], ACT.Sigmoid, bias=col("b_gate_2", b - 20))
                else:
                    take(("z", b), places[b], ACT.Sigmoid if 4 <= b < 8 else ACT.Copy)
                if b % 4 == 2 and b // 4 + 2 < PARTED_Z:
                    part()
                if b == 20:
                    act.wait_ge(S("ple_mm"), 1)
                    act.activation(pleT.rearrange("p a b -> p (a b)"), BK[7], ACT.Copy).then_inc(S("pleT"), 1)
                if b == 32:
                    act.wait_ge(S("ln_mean"), 1)
                    act.activation(sq[:, 0:CC, :], acc[:, :, :], ACT.Square).then_inc(S("ln_sq"), 1)

            act.wait_ge(S("ln_ss"), 1)
            inverse_root(stat[:, 0, :], BK[5][:, 0:T], 512, "ln_std")
            for b in range(CC):
                act.wait_ge(S("ln_norm"), b + 1)
                act.activation(acc[:, b, :], acc[:, b, :], ACT.Silu, bias=col("ln_a_b_2", b)).then_inc(S("branch_a"), 1)

            act.wait_ge(S("comb2"), KD)
            for k in range(KD):
                square_block("nff", k, "taken_V", taken_by("V", BLOCK_AT[("o", k)]))
                if k in (1, 6):
                    part()
            root("nff", D)
            part_h("nff")
            def ffn_gelu(b):
                act.wait_ge(S("conv_f"), b + 1)
                act.activation(fT[:, b, :], fT[:, b, :], ACT.Gelu_apprx_tanh,
                               bias=col("conv_f_b_2", b)).then_inc(S("ffn_gelu"), 1)

            for b in range(FB):
                if b == 0:
                    act.wait_ge(S("up_pads"), 1)
                take(("up", b), upad[:, b, 2:])
                if b % 4 == 2:
                    part()
                if b >= 2:
                    ffn_gelu(b - 2)
            ffn_gelu(FB - 2)
            ffn_gelu(FB - 1)
            def part_f(b):
                act.wait_ge(S("taken_V"), taken_by("V", BLOCK_AT[("up", FB + b)]))
                act.activation(f_hi[:, b, :], fT[:, b, :], ACT.Copy).then_inc(S("f_hi"), 1)

            for b in range(FB):
                if b % 4 == 0:
                    part()
                part_f(b)
            for j in range(4):
                part()
                part()
                for b in range(2):
                    square_block("np", 2 * j + b, "taken_V", taken_by("V", BLOCK_AT[("down", 2 * j + b)]))
            root("np", D)
            part_h("np")
            for b in range(8):
                take(("pg", b), pgT[:, b, :], ACT.Sigmoid)
            squares("nl", "x5")
            root("nl", D)
            for i in range(2):
                for t in range(NT):
                    act.wait_ge(S("out_mm"), 2 * i + t + 1)
                    act.activation(otok[:, t, i * 512:(i + 1) * 512], BK[4 + 2 * t + i], ACT.Copy).then_inc(S("out_cp"), 1)

        @block.vector
        def _(v):
            n_of = {}

            def link(ins, name="vec_step"):
                n_of[name] = n_of.get(name, 0) + 1
                ins.then_inc(S(name), 1)
                v.wait_ge(S(name), n_of[name])

            def stt(out, in0, scalar, in1, op0=ALU.mult, op1=ALU.mult):
                return v.scalar_tensor_tensor(out=out, in0=in0, scalar=scalar, in1=in1, op0=op0, op1=op1)

            taken = [0]

            def arrived(key):
                b = BLOCK_AT[key]
                assert BLOCKS[b][1] == "V" and taken_by("V", b) == taken[0] + 1, key
                taken[0] += 1
                v.wait_ge(S("product"), b + 1)
                return BK[b % BANKS]

            def ada_part(j, ks=range(KD)):
                c = chunk_of(BLOCK_AT[("ada", j)])
                if ks[0] == 0:
                    v.wait_ge(S(f"chunk{c % SLOTS}"), 16 * (c // SLOTS + 1))
                wt, part = wring[:, c % SLOTS, 0:KD * 512].rearrange("p (k n) -> p k n", n=512), ada_sum[:, j % 2, :]
                for k in ks:
                    if k == 0:
                        ins = v.tensor_scalar(part, wt[:, 0, :], csil[:, 0:1], None, ALU.mult)
                    else:
                        ins = stt(part, wt[:, k, :], csil[:, k:k + 1], part, ALU.mult, ALU.add)
                    link(ins, "ada_sum" if k == KD - 1 else "vec_step")

            def ada(j):
                bank = arrived(("ada", j))
                link(v.tensor_tensor(adaT[:, 4 * j:4 * j + 4], bank[:, 0:4], cols("b_ada", 48)[:, 4 * j:4 * j + 4],
                                     ALU.add), "taken_V")

            def normed(tag, out, gain, n=KD, src=xT, signal="_h"):
                v.wait_ge(S(tag + "_std"), 1)
                for k in range(n):
                    ins = stt(out[:, k, :], src[:, k, :], gain(k), stat[:, 1, :])
                    if n == KD:
                        ins.then_inc(S(tag + signal), 1)
                if n == KD:
                    v.wait_ge(S(tag + signal), n)
                else:
                    link(ins, tag + signal)

            v.wait_ge(S("vec_mm"), 1)
            link(v.tensor_copy(vec[:, 0, 0:ROW_TILES[0]], BK[5][:, 0:ROW_TILES[0]]), "vec")
            v.wait_ge(S("csil"), 1)
            ada_part(0)
            for b in range(4):
                v.wait_ge(S("x_mm"), b + 1)
                link(v.tensor_copy(xT[:, 2 * b:2 * b + 2, :], BK[4 + b].rearrange("p (a b) -> p a b", b=T)), "xT")
            ada_part(1)
            ada(0)
            for j in range(2, 4):
                ada_part(j)
                ada(j - 1)
            ada(3)
            link(stt(mod[:, :], adaT[:, 8:16], 1.0, cols("norm1_g", KD), ALU.add, ALU.mult))
            for k in range(KD):
                v.wait_ge(S("n1_x"), k + 1)
                ins = v.tensor_scalar(hT[:, k, :], hT[:, k, :], mod[:, k:k + 1], adaT[:, k:k + 1], ALU.mult, ALU.add)
                ins.then_inc(S("n1_h"), 1)
            v.wait_ge(S("n1_h"), KD)
            v.wait_ge(S("vec_late_mm"), 1)
            for i in range(1, 4):
                ins = v.tensor_copy(vec[:, i, 0:ROW_TILES[i]], BK[6][:, i * P:i * P + ROW_TILES[i]])
            link(ins)
            v.wait_ge(S("vec_late_mm"), 2)
            link(v.tensor_copy(keyT[:, :, :], BK[7][:, 0:2 * P].rearrange("p (a b) -> p a b", b=P)), "keyT")

            v.wait_ge(S("gate_ln"), 1)
            v.wait_ge(S("pool_consts"), 1)
            link(v.tensor_scalar(la, la, 0.0, None, ALU.min))
            link(v.tensor_tensor(la, la, cum, ALU.subtract))
            for h in range(GH):
                ins = v.tensor_tensor_scan(cum[:, h * T:(h + 1) * T], scanmask, la[:, h * T:(h + 1) * T], 0.0,
                                           ALU.mult, ALU.add)
            link(ins)
            by_chunk = [a.rearrange("p (n c) -> p n c", c=CH) for a in (cum, ediff, ework)]
            link(v.tensor_tensor(by_chunk[1], by_chunk[0][:, :, CH - 1:CH].broadcast_to([P, 4 * GH, CH]), by_chunk[0],
                                 ALU.subtract), "gate_sum")
            normed("kv", kvT, lambda k: col("dsa_kv_norm_g", k), n=2, src=kvT)
            v.wait_ge(S("gate_exp"), 1)
            v.wait_ge(S("taken_A"), taken_by("A", BLOCK_AT[("gk", 3)]))
            flat = lambda a: a.rearrange("p a b -> p (a b)")
            v.tensor_copy(decay.rearrange("p (n c) -> p n c", c=1), by_chunk[2][:, :, CH - 1:CH])
            stt(flat(gq), flat(gq), DK ** -0.5, ework)
            v.tensor_tensor(ediff, flat(gk), ediff, ALU.mult)
            link(v.tensor_tensor(flat(gk), flat(gk), la, ALU.mult), "gla_in")
            v.wait_ge(S("ckv_mm"), 1)
            link(v.tensor_copy(ckv_tok[:, :, :], BK[5].rearrange("p (a b) -> p a b", b=LAT)), "ckv_tok")

            v.wait_ge(S("taken_A"), taken_by("A", BLOCK_AT[("iw", NT - 1)]))
            v.wait_ge(S("gate_mm"), 1)
            for t in range(NT):
                nk = P * (t + 1)
                if t:
                    v.wait_ge(S("causal"), t)
                for h in range(IH):
                    i = t * IH + h
                    v.wait_ge(S("rel"), i + 1)
                    if h == 0:
                        ins = v.tensor_scalar(score[:, 0:nk], rel[:, i % 2, 0:nk], iw[:, t, h:h + 1], None, ALU.mult)
                    else:
                        ins = stt(score[:, 0:nk], rel[:, i % 2, 0:nk], iw[:, t, h:h + 1], score[:, 0:nk],
                                  ALU.mult, ALU.add)
                    link(ins, "index_sum")
                v.wait_ge(S("causal"), t + 1)
                for r in range(TOPK // 8):
                    link(v.max(m8, work[:, 0:nk]))
                    link(v.match_replace(work[:, 0:nk], m8, work[:, 0:nk], TAKEN))
                link(v.tensor_scalar(madd[:, t, 0:nk], work[:, 0:nk], 0.5 * TAKEN, OUT_OF, ALU.is_ge, ALU.mult), "picked")

            for n in range(3):
                v.wait_ge(S("update_mm"), n + 1)
                for h in range(GH):
                    u = BK[6 + h // 2][:, (h % 2) * DV:(h % 2 + 1) * DV]
                    if n == 0:
                        ins = v.tensor_copy(state[:, 0, h, :], u)
                    else:
                        ins = stt(state[:, n, h, :], state[:, n - 1, h, :], decay[:, 4 * h + n:4 * h + n + 1], u,
                                  ALU.mult, ALU.add)
                link(ins, "state")
            v.wait_ge(S("o_std"), 1)
            for b in range(8):
                ins = stt(oT[:, b, :], oT[:, b, :], col("gla_norm_g", b), ostd[:, (b // 2) * T:(b // 2 + 1) * T])
            link(ins, "o_normed")

            v.wait_ge(S("madd_ready"), NT)
            for h in range(AH):
                ada_part(4 + h, range(KD // 2))
                for t in range(NT):
                    nk = P * (t + 1)
                    ins = stt(rel[:, t, 0:nk], negdist[:, t, 0:nk], 2.0 ** -(h + 1), madd[:, t, 0:nk], ALU.mult, ALU.add)
                link(ins)
                v.wait_ge(S("logit_mm"), h + 1)
                for t in range(NT):
                    nk = P * (t + 1)
                    ins = stt(pr[:, t, 0:nk], BK[5][:, t * P:t * P + nk], P ** -0.5, rel[:, t, 0:nk], ALU.mult, ALU.add)
                link(ins)
                for t in range(NT):
                    ins = v.tensor_reduce(sm[:, t:t + 1], pr[:, t, 0:P * (t + 1)], X, ALU.max)
                link(ins)
                link(v.tensor_scalar(sm[:, 2:4], sm[:, 0:2], -1.0, None, ALU.mult), "logits")
                v.wait_ge(S("p_exp"), h + 1)
                link(v.reciprocal(sm[:, 6:8], sm[:, 4:6]))
                for t in range(NT):
                    nk = P * (t + 1)
                    ins = v.tensor_scalar(pr[:, t, 0:nk], pr[:, t, 0:nk], sm[:, 6 + t:7 + t], None, ALU.mult)
                link(ins, "p_ready")
                ada_part(4 + h, range(KD // 2, KD))
                ada(4 + h)
                v.wait_ge(S("dsa_mm"), h + 1)
                link(v.tensor_copy(dsaT[:, h, :], BK[4][:, 0:T]), "dsa_cp")

            v.wait_ge(S("gates"), 1)
            for b in range(8):
                link(v.tensor_tensor(comb[:, b, :], arrived(("ba", b))[:, 0:T], za[:, b, :], ALU.mult), "taken_V")
            for b in range(8):
                link(v.tensor_tensor(zb[:, b, :], arrived(("bb", b))[:, 0:T], zb[:, b, :], ALU.mult), "taken_V")
                link(v.tensor_tensor(comb[:, b, :], comb[:, b, :], zb[:, b, :], ALU.add), "comb")
            for b in range(8):
                link(stt(xT[:, b, :], arrived(("wo", b))[:, 0:T], adaT[:, 16 + b:17 + b], xT[:, b, :], ALU.mult, ALU.add),
                     "taken_V")
            link(stt(mod[:, :], adaT[:, 32:40], 1.0, cols("norm2_g", KD), ALU.add, ALU.mult))
            normed("n2", hT, lambda k: mod[:, k:k + 1], signal="_scaled")

            def by(body):
                n = [0]

                def step(ins):
                    n[0] += 1
                    ins.then_inc(S("head_step"), 1)
                    v.wait_ge(S("head_step"), n[0])

                body(step)
                v.sem_inc(S("head_step"), -n[0])

            def route(g, even):
                def body(step):
                    step(v.tensor_copy(cur, s_all[:, bass.ds(g, 1), :].rearrange("p a b -> p (a b)")
                                       if not isinstance(g, int) else s_all[:, g, :]))
                    for i in range(2):
                        half, half2 = cur[:, i * NKEY:(i + 1) * NKEY], cur2[:, i * NKEY:(i + 1) * NKEY]
                        step(v.max(top[:, i, 0:8], half))
                        v.max_index(topu[:, i, 0:8], top[:, i, 0:8], half)
                        step(v.match_replace(half2, top[:, i, 0:8], half, TAKEN))
                        step(v.max(top[:, i, 8:16], half2))
                        step(v.max_index(topu[:, i, 8:16], top[:, i, 8:16], half2))
                    v.tensor_copy(topi[:, :, :], topu[:, :, :])
                    step(v.tensor_tensor(cand, top[:, 0, :].rearrange("p (a b) -> p a b", b=1).broadcast_to([P, EK, EK]),
                                         top[:, 1, :].rearrange("p (b a) -> p b a", b=1).broadcast_to([P, EK, EK]),
                                         ALU.add))
                    cf, cf2 = cand.rearrange("p a b -> p (a b)"), cand2.rearrange("p a b -> p (a b)")
                    step(v.max(best[:, 0:8], cf))
                    v.max_index(ciu[:, 0, 0:8], best[:, 0:8], cf)
                    step(v.match_replace(cf2, best[:, 0:8], cf, TAKEN))
                    step(v.max(best[:, 8:16], cf2))
                    step(v.max_index(ciu[:, 0, 8:16], best[:, 8:16], cf2))
                    v.tensor_scalar(gst[:, 0:1], best[:, 0:1], -1.0, None, ALU.mult).then_inc(S("best"), 1)
                    v.tensor_scalar(ciu[:, 1, :], ciu[:, 0, :], 4, None, ALU.logical_shift_right)
                    step(v.tensor_scalar(ciu[:, 2, :], ciu[:, 0, :], EK - 1, None, ALU.bitwise_and))
                    step(v.tensor_copy(ci[:, :, :], ciu[:, 1:3, :]))
                    for i in range(2):
                        step(v.tensor_tensor(oneh, iota16[:, :].rearrange("p (b a) -> p b a", b=1).broadcast_to([P, EK, EK]),
                                             ci[:, i, :].rearrange("p (a b) -> p a b", b=1).broadcast_to([P, EK, EK]),
                                             ALU.is_equal))
                        step(v.tensor_tensor(oneh, oneh,
                                             topi[:, i, :].rearrange("p (b a) -> p b a", b=1).broadcast_to([P, EK, EK]),
                                             ALU.mult))
                        step(v.tensor_reduce(pick[:, i, :], oneh, X, ALU.add))
                    step(stt(pick[:, 0, :], pick[:, 0, :], float(NKEY), pick[:, 1, :], ALU.mult, ALU.add))
                    v.tensor_copy(rowid[:, even, :], pick[:, 0, :]).then_inc(S("rows_ready"), 1)
                by(body)

            def dot(g, even, t, q):
                v.wait_ge(S(f"u_in{q}"), 16 * PER_Q * (g + 1))
                v.sem_inc(S("tick"), 1)
                for j in range(PER_Q * q, PER_Q * (q + 1)):
                    v.tensor_tensor_reduce(out=urows[:, j, :], in0=urows[:, j, :], in1=h2tok[:, t, :], scale=1.0,
                                           scalar=0.0, op0=ALU.mult, op1=ALU.add,
                                           accum_out=dots[:, even, j:j + 1]).then_inc(S("dot"), 1)

            def weigh(g, even):
                v.wait_ge(S("best_exp"), g + 1)
                v.sem_inc(S("tick"), 1)
                by(lambda step: step(v.reciprocal(gst[:, 2:3], gst[:, 1:2])))
                v.wait_ge(S("gelu"), g + 1)
                v.sem_inc(S("tick"), 1)
                stt(amul[:, even, :], gel, gst[:, 2:3], expb).then_inc(S("weight"), 1)

            def add(g, even, t):
                v.wait_ge(S("v_used"), EK * (g + 1))
                v.sem_inc(S("tick"), 1)
                v.wait_ge(S("head_added"), g + 1)
                acc_t = pacc[:, t, :].rearrange("p (a b) -> p a b", b=512)
                v.tensor_tensor(acc_t, ps[:, 4 + 2 * even:6 + 2 * even, :], acc_t, ALU.add).then_inc(S("head_added"), 1)

            def head(g, even, t, last=False, add_to=None):
                for q in range(QUARTERS):
                    dot(g, even, t, q)
                add(g - 1, 1 - even, t if add_to is None else add_to)
                weigh(g, even)
                if not last:
                    route(g + 1, 1 - even)

            v.memset(s_all[:, NT * EH, :], 0.0)
            link(v.memset(pacc[:, :, :], 0.0), "head_added")

            def scores(h):
                v.wait_ge(S("score_mm"), h + 1)
                link(v.tensor_copy(s_all[:, h:h + EH + 1:EH, :], BK[4 + h % 4].rearrange("p (t n) -> p t n", n=2 * NKEY)),
                     "scores")

            scores(0)
            route(0, 0)
            scores(1)
            scores(2)
            v.wait_ge(S("best_exp"), 1)
            route(1, 1)
            scores(3)
            v.wait_ge(S("h2tok"), 4)
            for q in range(QUARTERS):
                scores(4 + q)
                dot(0, 0, 0, q)
            weigh(0, 0)
            with v.Fori(1, EH - 1, 2) as g:
                head(g, 1, 0)
                head(g + 1, 0, 0)
            head(EH - 1, 1, 0)
            head(EH, 0, 1, add_to=0)
            with v.Fori(EH + 1, 2 * EH - 1, 2) as g:
                head(g, 1, 1)
                head(g + 1, 0, 1)
            head(2 * EH - 1, 1, 1, last=True)
            add(2 * EH - 1, 1, 1)
            for b in range(4):
                v.wait_ge(S("expert_mm"), b + 1)
                for k in (2 * b, 2 * b + 1):
                    ins = stt(xT[:, k, :], BK[4 + b][:, (k % 2) * T:(k % 2 + 1) * T], adaT[:, 40 + k:41 + k],
                              xT[:, k, :], ALU.mult, ALU.add)
                    link(ins, "expert_x")
            normed("nf1", xT, lambda k: col("final_norm_g", k))

            normed("nm", hT, lambda k: col("g_mix_2", k))
            v.wait_ge(S("taken_A"), taken_by("A", BLOCK_AT[("z", 7)]))
            v.memset(apad[:, :, 0:CK - 1], 0.0)
            v.memset(cpad[:, :, 0:2], 0.0)
            link(v.tensor_tensor(apad[:, :, CK - 1:], apad[:, :, CK - 1:], agate[:, :, :], ALU.mult))
            for tap in range(CK):
                for b in range(CC):
                    wcol = col("conv_a_w_2", tap * CC + b)
                    if tap == 0:
                        ins = v.tensor_scalar(acc[:, b, :], apad[:, b, 0:T], wcol, col("conv_a_b_2", b), ALU.mult, ALU.add)
                    else:
                        ins = stt(acc[:, b, :], apad[:, b, tap:tap + T], wcol, acc[:, b, :], ALU.mult, ALU.add)
                link(ins, "conv_a" if tap == CK - 1 else "vec_step")
            v.wait_ge(S("ln_sum"), 1)
            link(v.tensor_scalar(stat[:, 1, :], BK[4][:, 0:T], 1.0 / 512, None, ALU.mult))
            for b in range(CC):
                ins = v.tensor_tensor(acc[:, b, :], acc[:, b, :], stat[:, 1, :], ALU.subtract)
            link(ins, "ln_mean")
            v.wait_ge(S("taken_A"), taken_by("A", BLOCK_AT[("z", 19)]))
            link(v.tensor_tensor(cpad[:, :, 2:], cpad[:, :, 2:], scc[:, :, :], ALU.mult))
            for tap in range(3):
                for b in range(CC):
                    wcol = col("conv_b_w_2", tap * CC + b)
                    if tap == 0:
                        ins = v.tensor_scalar(sT[:, b, :], cpad[:, b, 0:T], wcol, None, ALU.mult)
                    else:
                        ins = stt(sT[:, b, :], cpad[:, b, tap:tap + T], wcol, sT[:, b, :], ALU.mult, ALU.add)
                link(ins)
            link(v.tensor_tensor(sT[:, :, :], sT[:, :, :], scb[:, :, :], ALU.mult), "conv_b")
            v.wait_ge(S("ln_std"), 1)
            for b in range(CC):
                link(stt(acc[:, b, :], acc[:, b, :], col("ln_a_g_2", b), stat[:, 0, :]), "ln_norm")
            v.wait_ge(S("taken_A"), taken_by("A", BLOCK_AT[("z", 35)]))
            for b in range(8):
                link(v.tensor_tensor(comb2[:, b, :], arrived(("yb", b))[:, 0:T], zg[:, 8 + b, :], ALU.mult), "taken_V")
            for b in range(8):
                link(v.tensor_tensor(zg[:, b, :], arrived(("ya", b))[:, 0:T], zg[:, b, :], ALU.mult), "taken_V")
                link(v.tensor_tensor(comb2[:, b, :], comb2[:, b, :], zg[:, b, :], ALU.add), "comb2")

            def residual(key):
                for b in range(8):
                    link(v.tensor_tensor(xT[:, b, :], arrived((key, b))[:, 0:T], xT[:, b, :], ALU.add), "taken_V")

            link(v.memset(upad[:, :, 0:2], 0.0), "up_pads")
            residual("o")
            normed("nff", hT, lambda k: col("g_ffn_2", k))
            for b in range(FB):
                v.wait_ge(S("taken_A"), taken_by("A", BLOCK_AT[("up", b)]))
                for tap in range(3):
                    wcol = col("conv_f_w_2", tap * FB + b)
                    if tap == 0:
                        ins = v.tensor_scalar(fT[:, b, :], upad[:, b, 0:T], wcol, None, ALU.mult)
                    else:
                        ins = stt(fT[:, b, :], upad[:, b, tap:tap + T], wcol, fT[:, b, :], ALU.mult, ALU.add)
                    link(ins, "conv_f" if tap == 2 else "vec_step")
            def rest_of_f(b):
                v.wait_ge(S("f_hi"), b + 1)
                ins = v.tensor_tensor(f_lo[:, b, :], fT[:, b, :], f_hi[:, b, :].bitcast(F32), ALU.subtract)
                ins.then_inc(S("f_lo"), 1)

            for b in range(FB):
                v.wait_ge(S("ffn_gelu"), b + 1)
                ins = v.tensor_tensor(fT[:, b, :], arrived(("up", FB + b))[:, 0:T], fT[:, b, :], ALU.mult)
                link(ins, "taken_V")
                if b:
                    rest_of_f(b - 1)
            rest_of_f(FB - 1)
            residual("down")
            normed("np", hT, lambda k: col("g_ple_2", k))
            for b in range(8):
                bank = arrived(("pl", b))
                if b == 0:
                    v.wait_ge(S("taken_A"), taken_by("A", BLOCK_AT[("pg", 7)]))
                link(v.tensor_tensor(pgT[:, b, :], bank[:, 0:T], pgT[:, b, :], ALU.mult), "taken_V")
                ins = v.tensor_tensor(xT[:, b, :], xT[:, b, :], pgT[:, b, :], ALU.add)
                link(ins, "x5")
            normed("nl", hT, lambda k: col("g_final_2", k))


def kernel(**inputs):
    import numpy as np
    import concourse.bacc as bacc
    from concourse.bass_utils import run_bass_kernel_spmd

    nc = bacc.Bacc("TRN2", target_bir_lowering=False, num_devices=1)
    arrays, w = {}, {}
    for name in INPUTS:
        a = np.ascontiguousarray(inputs[name])
        arrays["in_" + name] = a
        w[name] = nc.dram_tensor("in_" + name, a.shape, mybir.dt.from_np(a.dtype), kind="ExternalInput").ap()
    out = nc.dram_tensor("out_0", (1, T, D), F32, kind="ExternalOutput").ap()
    two_blocks(nc, w, out)
    r = run_bass_kernel_spmd(nc, [arrays], core_ids=[0])
    return r.results[0]["out_0"]
```
